# Optimizing a Trainium2 kernel written in Bass

```python
import jax, jax.numpy as jnp
from jax import lax
import numpy as np

D_MODEL = 2048
BATCH = 1
SEQ = 256
DEPTH = 2

N_A_LAYERS = DEPTH // 2
N_B_LAYERS = DEPTH - N_A_LAYERS

GLA_HEADS = 4
GLA_DK = D_MODEL // 2 // GLA_HEADS
GLA_DV = D_MODEL // GLA_HEADS
GLA_GATE_RANK = 16
GLA_GATE_NORM = 16.0
GLA_CHUNK = 64
GLA_IN = 2 * GLA_HEADS * GLA_DK + 2 * GLA_HEADS * GLA_DV + GLA_GATE_RANK

MLA_HEADS = D_MODEL // 128
MLA_Q_RANK = D_MODEL // 4
MLA_KV_RANK = D_MODEL // 4
MLA_NOPE = 128
MLA_ROPE = 64
MLA_V = 128
ROPE_THETA = 10000.0
ATTN_BLOCK = 128

D_FF = 5632
CONV_W = 3

EPS = 1e-6

kernel_name = "yoco_gla_mla_convffn_adaln"

def rmsnorm(x, g):
    xf = x.astype(jnp.float32)
    y = xf * lax.rsqrt(jnp.mean(xf * xf, axis=-1, keepdims=True) + EPS)
    return (y * g.astype(jnp.float32)).astype(x.dtype)

def modulate(h, shift, scale):
    return h * (1 + scale[:, None, :]) + shift[:, None, :]

def rope_tables(positions):
    inv = ROPE_THETA ** (-jnp.arange(0, MLA_ROPE, 2, dtype=jnp.float32) / MLA_ROPE)
    ang = positions.astype(jnp.float32)[..., None] * inv
    return jnp.cos(ang), jnp.sin(ang)

def apply_rope(x, cos, sin):
    xf = x.astype(jnp.float32)
    x1, x2 = jnp.split(xf, 2, axis=-1)
    return jnp.concatenate([x1 * cos - x2 * sin, x2 * cos + x1 * sin], axis=-1).astype(x.dtype)

def gla_chunked(q, k, v, log_a):
    B_, S_, H_, DK_ = q.shape
    DV_ = v.shape[-1]
    nc = S_ // GLA_CHUNK

    def to_chunks(t):
        d = t.shape[-1]
        return t.astype(jnp.float32).reshape(B_, nc, GLA_CHUNK, H_, d).transpose(1, 0, 3, 2, 4)

    qc, kc, vc, gc = to_chunks(q), to_chunks(k), to_chunks(v), to_chunks(log_a)
    tri = jnp.tril(jnp.ones((GLA_CHUNK, GLA_CHUNK), dtype=bool))

    def step(state, inp):
        qb, kb, vb, gb = inp
        b = jnp.cumsum(gb, axis=2)
        inter = jnp.einsum('bhid,bhdv->bhiv', qb * jnp.exp(b), state)
        diff = b[:, :, :, None, :] - b[:, :, None, :, :]
        decay = jnp.exp(jnp.where(tri[:, :, None], diff, -jnp.inf))
        scores = jnp.einsum('bhid,bhjd,bhijd->bhij', qb, kb, decay)
        intra = jnp.einsum('bhij,bhjv->bhiv', scores, vb)
        b_last = b[:, :, -1:, :]
        state = (jnp.exp(b_last[:, :, 0, :])[..., None] * state
                 + jnp.einsum('bhjd,bhjv->bhdv', kb * jnp.exp(b_last - b), vb))
        return state, inter + intra

    state0 = jnp.zeros((B_, H_, DK_, DV_), jnp.float32)
    _, out = lax.scan(step, state0, (qc, kc, vc, gc))
    return out.transpose(1, 0, 3, 2, 4).reshape(B_, S_, H_, DV_)

def gla_mixer(h, w_in, w_gate2, b_gate, head_g, w_o):
    B_, S_, _ = h.shape
    hk, hv = GLA_HEADS * GLA_DK, GLA_HEADS * GLA_DV
    proj = h @ w_in
    q, k, v, r, g1 = jnp.split(proj, [hk, 2 * hk, 2 * hk + hv, 2 * hk + 2 * hv], axis=-1)
    log_a = jax.nn.log_sigmoid((g1 @ w_gate2 + b_gate).astype(jnp.float32)) / GLA_GATE_NORM
    shp_k = (B_, S_, GLA_HEADS, GLA_DK)
    o = gla_chunked((q * GLA_DK ** -0.5).reshape(shp_k), k.reshape(shp_k),
                    v.reshape(B_, S_, GLA_HEADS, GLA_DV), log_a.reshape(shp_k))
    o = rmsnorm(o, head_g).astype(h.dtype)
    o = o * jax.nn.silu(r).reshape(B_, S_, GLA_HEADS, GLA_DV)
    return o.reshape(B_, S_, hv) @ w_o

def mla_shared_kv(x, c_act, kv_norm_g, kv_mod_w, kv_mod_b, w_dkv, kv_latent_g, w_ukv, cos, sin):
    B_, S_, _ = x.shape
    shift, scale = jnp.split(c_act @ kv_mod_w + kv_mod_b, 2, axis=-1)
    h = modulate(rmsnorm(x, kv_norm_g), shift, scale)
    ckv = h @ w_dkv
    latent, k_rope = ckv[..., :MLA_KV_RANK], ckv[..., MLA_KV_RANK:]
    kv = (rmsnorm(latent, kv_latent_g) @ w_ukv).reshape(B_, S_, MLA_HEADS, MLA_NOPE + MLA_V)
    k_nope, v = kv[..., :MLA_NOPE], kv[..., MLA_NOPE:]
    k_rope = apply_rope(k_rope, cos, sin)
    return k_nope, k_rope, v

def mla_attention(h, w_dq, q_norm_g, w_uq, w_o, k_nope, k_rope, v, cos, sin):
    B_, S_, _ = h.shape
    q = (rmsnorm(h @ w_dq, q_norm_g) @ w_uq).reshape(B_, S_, MLA_HEADS, MLA_NOPE + MLA_ROPE)
    q_nope = q[..., :MLA_NOPE]
    q_rope = apply_rope(q[..., MLA_NOPE:], cos[:, :, None, :], sin[:, :, None, :])
    scale = (MLA_NOPE + MLA_ROPE) ** -0.5
    outs = []
    for blk in range(S_ // ATTN_BLOCK):
        q0, q1 = blk * ATTN_BLOCK, (blk + 1) * ATTN_BLOCK
        s = (jnp.einsum('bqhd,bkhd->bhqk', q_nope[:, q0:q1], k_nope[:, :q1])
             + jnp.einsum('bqhr,bkr->bhqk', q_rope[:, q0:q1], k_rope[:, :q1]))
        s = s.astype(jnp.float32) * scale
        mask = jnp.arange(q1)[None, :] <= jnp.arange(q0, q1)[:, None]
        p = jax.nn.softmax(jnp.where(mask, s, -jnp.inf), axis=-1).astype(v.dtype)
        outs.append(jnp.einsum('bhqk,bkhv->bqhv', p, v[:, :q1]))
    o = jnp.concatenate(outs, axis=1).reshape(B_, S_, MLA_HEADS * MLA_V)
    return o @ w_o

def conv_ffn(h, w_up, conv_w, conv_b, w_down):
    u = h @ w_up
    u = lax.conv_general_dilated(
        u, conv_w[:, None, :].astype(u.dtype), window_strides=(1,), padding=[(CONV_W - 1, 0)],
        dimension_numbers=('NWC', 'WIO', 'NWC'), feature_group_count=u.shape[-1]) + conv_b
    val, gate = jnp.split(u, 2, axis=-1)
    return (jax.nn.silu(gate) * val) @ w_down

def setup_inputs(seed: int = 0) -> dict:
    key = jax.random.key(seed)
    ks = iter(jax.random.split(key, 40))
    f32 = jnp.float32

    def nrm(shape, scale):
        return jax.random.normal(next(ks), shape, f32) * scale

    def gain(shape):
        return 1.0 + nrm(shape, 0.01)

    D = D_MODEL
    x = nrm((BATCH, SEQ, D), 1.0)
    c = nrm((BATCH, D), 1.0)
    offset = jax.random.randint(next(ks), (BATCH, 1), 0, 4096, dtype=jnp.int32)
    positions = offset + jnp.arange(SEQ, dtype=jnp.int32)[None, :]
    return {
        "x": x,
        "c": c,
        "positions": positions,
        "mod_w": nrm((DEPTH, D, 6 * D), 0.5 * D ** -0.5),
        "mod_b": nrm((DEPTH, 6 * D), 0.01),
        "norm_mix_g": gain((DEPTH, D)),
        "norm_ffn_g": gain((DEPTH, D)),
        "gla_w_in": nrm((N_A_LAYERS, D, GLA_IN), D ** -0.5),
        "gla_w_gate2": nrm((N_A_LAYERS, GLA_GATE_RANK, GLA_HEADS * GLA_DK), GLA_GATE_RANK ** -0.5),
        "gla_b_gate": nrm((N_A_LAYERS, GLA_HEADS * GLA_DK), 0.01),
        "gla_head_g": gain((N_A_LAYERS, GLA_HEADS, GLA_DV)),
        "gla_w_o": nrm((N_A_LAYERS, GLA_HEADS * GLA_DV, D), (GLA_HEADS * GLA_DV) ** -0.5),
        "kv_norm_g": gain((D,)),
        "kv_mod_w": nrm((D, 2 * D), 0.5 * D ** -0.5),
        "kv_mod_b": nrm((2 * D,), 0.01),
        "mla_w_dkv": nrm((D, MLA_KV_RANK + MLA_ROPE), D ** -0.5),
        "mla_kv_norm_g": gain((MLA_KV_RANK,)),
        "mla_w_ukv": nrm((MLA_KV_RANK, MLA_HEADS * (MLA_NOPE + MLA_V)), MLA_KV_RANK ** -0.5),
        "mla_w_dq": nrm((N_B_LAYERS, D, MLA_Q_RANK), D ** -0.5),
        "mla_q_norm_g": gain((N_B_LAYERS, MLA_Q_RANK)),
        "mla_w_uq": nrm((N_B_LAYERS, MLA_Q_RANK, MLA_HEADS * (MLA_NOPE + MLA_ROPE)), MLA_Q_RANK ** -0.5),
        "mla_w_o": nrm((N_B_LAYERS, MLA_HEADS * MLA_V, D), (MLA_HEADS * MLA_V) ** -0.5),
        "ffn_w_up": nrm((DEPTH, D, 2 * D_FF), D ** -0.5),
        "ffn_conv_w": nrm((DEPTH, CONV_W, 2 * D_FF), CONV_W ** -0.5),
        "ffn_conv_b": nrm((DEPTH, 2 * D_FF), 0.01),
        "ffn_w_down": nrm((DEPTH, D_FF, D), D_FF ** -0.5),
        "final_norm_g": gain((D,)),
    }

def reference(x, c, positions, mod_w, mod_b, norm_mix_g, norm_ffn_g,
              gla_w_in, gla_w_gate2, gla_b_gate, gla_head_g, gla_w_o,
              kv_norm_g, kv_mod_w, kv_mod_b, mla_w_dkv, mla_kv_norm_g, mla_w_ukv,
              mla_w_dq, mla_q_norm_g, mla_w_uq, mla_w_o,
              ffn_w_up, ffn_conv_w, ffn_conv_b, ffn_w_down, final_norm_g):
    c_act = jax.nn.silu(c)
    cos, sin = rope_tables(positions)
    shared_kv = None
    for i in range(DEPTH):
        mod = c_act @ mod_w[i] + mod_b[i]
        sh_m, sc_m, g_m, sh_f, sc_f, g_f = jnp.split(mod, 6, axis=-1)
        h = modulate(rmsnorm(x, norm_mix_g[i]), sh_m, sc_m)
        if i < N_A_LAYERS:
            j = i
            y = gla_mixer(h, gla_w_in[j], gla_w_gate2[j], gla_b_gate[j], gla_head_g[j], gla_w_o[j])
        else:
            if i == N_A_LAYERS:
                shared_kv = mla_shared_kv(x, c_act, kv_norm_g, kv_mod_w, kv_mod_b,
                                          mla_w_dkv, mla_kv_norm_g, mla_w_ukv, cos, sin)
            j = i - N_A_LAYERS
            k_nope, k_rope, v = shared_kv
            y = mla_attention(h, mla_w_dq[j], mla_q_norm_g[j], mla_w_uq[j], mla_w_o[j],
                              k_nope, k_rope, v, cos, sin)
        x = x + (1 + g_m)[:, None, :] * y
        h = modulate(rmsnorm(x, norm_ffn_g[i]), sh_f, sc_f)
        x = x + (1 + g_f)[:, None, :] * conv_ffn(h, ffn_w_up[i], ffn_conv_w[i], ffn_conv_b[i], ffn_w_down[i])
    return rmsnorm(x, final_norm_g)


_drawn_inputs = setup_inputs


def setup_inputs(seed=0):
    import zlib

    import numpy as np

    out = dict(_drawn_inputs(seed))
    spreads = {}
    factors = {'norm_mix_g': 4.12,
     'norm_ffn_g': 5.469,
     'gla_b_gate': 8.0,
     'gla_head_g': 8.0,
     'kv_norm_g': 27.153,
     'kv_mod_b': 7.426,
     'mla_kv_norm_g': 34.109,
     'mla_q_norm_g': 28.005,
     'ffn_conv_b': 5.716,
     'final_norm_g': 33.446}
    for name, (base, spread) in spreads.items():
        noise = np.random.default_rng([zlib.crc32(name.encode()), seed]).standard_normal(out[name].shape)
        drawn = base * np.exp(spread * noise) if base else spread * noise
        out[name] = __import__('jax').numpy.asarray(drawn.astype(out[name].dtype))
    for name, factor in factors.items():
        out[name] = (out[name] * factor).astype(out[name].dtype)
    return out
```

```python
from contextlib import ExitStack, contextmanager

import concourse.bass as bass
from concourse import mybir

ALU = mybir.AluOpType
ACT = mybir.ActivationFunctionType
F32 = mybir.dt.float32
F32R = mybir.dt.float32r
I32 = mybir.dt.int32
I8 = mybir.dt.int8
AX_X = mybir.AxisListType.X

P = 128
RAW = 4
AHEAD = 2
MODS = 2
KT_ITEM = 4
W = 512
ITEM = KT_ITEM * W
EPS = 1e-6
NEG = -3.0e38
TWO_PI = 6.283185307179586
SPLIT_2PI = (6.28125, round((TWO_PI - 6.28125) * 2 ** 21) / 2 ** 21)
ROUND = 1.5 * 2.0 ** 23

UP_BLOCKS = (4, 4, 3)


def sections():
    s = [
        ("setup", 1, 0, 0, 0, 3, 0),
        ("pre", 1, 0, 32, 0, 0, 2),
        ("norm0", 1, 0, 0, 0, 8, 0),
        ("gate", 1, 1, 0, 0, 1, 9),
        ("qk", 2, 8, 8, 2, 4, 0),
        ("diag", 1, 0, 0, 0, 0, 2),
        ("v", 1, 16, 16, 4, 0, 16),
        ("mod_v", 1, 0, 0, 0, 0, 5),
        ("r", 2, 8, 0, 2, 0, 0),
        ("o", 1, 0, 0, 0, 8, 0),
        ("gla_out", 2, 8, 8, 2, 0, 0),
        ("mod_gla", 1, 0, 0, 0, 0, 1),
        ("norm1", 1, 0, 0, 0, 8, 0),
    ]

    def ffn(layer, up_mods, down_mods, after_up, after_down):
        for g, n in enumerate(UP_BLOCKS):
            s.append((f"up{layer}{g}", n, 8, up_mods[g], 2, 4, 0))
            s.append((f"modu{layer}{g}", 1, 0, 0, 0, 0, after_up[g]))
            s.append((f"down{layer}{g}", 2, 8, down_mods[g], 2, 0, 0))
            s.append((f"modd{layer}{g}", 1, 0, 0, 0, 0, after_down[g]))

    ffn(0, (4, 4, 0), (8, 8, 8), (4, 1, 0), (1, 1, 1))
    s += [
        ("norm2", 1, 0, 0, 0, 8, 0),
        ("latent", 1, 9, 0, 2, 0, 1),
        ("norm3", 1, 0, 0, 0, 2, 0),
        ("norm4", 1, 0, 0, 0, 2, 0),
        ("krope", 1, 0, 0, 0, 1, 0),
        ("ukv", 1, 8, 16, 8, 8, 0),
        ("mod_ukv", 1, 0, 0, 0, 0, 4),
        ("uq", 1, 8, 16, 8, 16, 0),
        ("mod_uq", 1, 0, 0, 0, 0, 1),
        ("heads", 1, 0, 0, 0, 16, 32),
        ("mla_out", 2, 8, 8, 2, 0, 0),
        ("mod_mla", 1, 0, 0, 0, 0, 1),
        ("norm5", 1, 0, 0, 0, 8, 0),
    ]
    ffn(1, (4, 0, 0), (0, 0, 0), (4, 0, 0), (0, 0, 0))
    return s


class At:

    def __init__(self, counts, n):
        self.item, self.mod, self.chunk, self.tp, self.ms = counts
        self.n = n


def table():
    at, counts = {}, [0] * 5
    for name, n, *per in sections():
        at[name] = At(counts, n)
        counts = [c + n * p for c, p in zip(counts, per)]
    at["end"] = At(counts, 0)
    return at


class Steps:

    def __init__(self, eng, sem):
        self.eng, self.sem, self.base, self.n = eng, sem, 0, 0

    def mark(self, ins):
        ins.then_inc(self.sem, 1)
        self.n += 1
        return self.base + self.n

    def wait(self, value):
        self.eng.wait_ge(self.sem, value)

    def link(self, ins):
        self.wait(self.mark(ins))

    @contextmanager
    def loop(self, i, start, end, per):
        first = self.base + self.n
        self.base, self.n = first + (i - start) * per, 0
        yield
        assert self.n == per, (self.n, per)
        self.base, self.n = first + (end - start) * per, 0


def yoco_kernel(nc, x, c, positions, mod_w, mod_b, norm_mix_g, norm_ffn_g, gla_w_in, gla_w_gate2,
                gla_b_gate, gla_head_g, gla_w_o, kv_norm_g, kv_mod_w, kv_mod_b, mla_w_dkv,
                mla_kv_norm_g, mla_w_ukv, mla_w_dq, mla_q_norm_g, mla_w_uq, mla_w_o, ffn_w_up,
                ffn_conv_w, ffn_conv_b, ffn_w_down, final_norm_g, out):
    _, T, D = x.shape
    TT = T // P
    KT = D // P
    HEADS = gla_head_g.shape[1]
    DV = gla_head_g.shape[2]
    RANK = gla_w_gate2.shape[1]
    HK = gla_w_gate2.shape[2]
    DKT = HK // P
    DK = HK // HEADS
    GATE_NORM = 16.0
    LAT = mla_w_ukv.shape[0]
    LT = LAT // P
    MH = D // P
    ROPE = mla_w_dkv.shape[1] - LAT
    HR = ROPE // 2
    FF = ffn_w_down.shape[1]
    FT = FF // P
    MSCALE = float(P + ROPE) ** -0.5
    assert TT == 2 and KT == 16 and DKT == 8 and LT == 4 and DV == W and sum(UP_BLOCKS) * W == FF
    assert DK ** -0.5 == 0.25 * 0.25
    at = table()
    TOTAL = at["end"].item

    base = (nc.sbuf_base + 63) // 64 * 64

    def place(name, offset, shape, dt):
        return nc.alloc_sbuf_tensor_at(name, shape, dt, offset=base + offset)

    K16 = 16384
    X, S1, S2, RW, MD, WS, AC, GU, PR = 0, K16, 3 * K16, 5 * K16, 7 * K16, 8 * K16, 10 * K16, 11 * K16, 12 * K16
    x_sb = place("x_sb", X, [P, TT, D], F32)
    h_hi = place("h_hi", S1, [P, KT, T], F32R)
    h_lo = place("h_lo", S1 + K16, [P, KT, T], F32R)
    a_hi = place("a_hi", S2, [P, KT, T], F32R)
    a_lo = place("a_lo", S2 + K16, [P, KT, T], F32R)
    raw = place("raw", RW, [P, RAW, ITEM], F32)
    mods = place("mods", MD, [P, MODS, D], F32)
    w_hi = place("w_hi", WS, [P, AHEAD, ITEM], F32R)
    w_lo = place("w_lo", WS + K16, [P, AHEAD, ITEM], F32R)
    acc = place("acc", AC, [P, 2, D], F32)
    gate_b = place("gate_b", GU, [P, D], F32)
    u = place("u", GU + 8192, [P, 2, TT, W], F32)
    xn = place("xn", GU, [P, TT, D], F32)
    prow = place("prow", S2, [P, 3, P], F32)
    crow = place("crow", S2 + 2048, [KT, 2, P], F32)
    cvrow = place("cvrow", S2 + 4096, [2 * FT, 8, P], F32)
    qk_t = place("qk_t", X, [P, 2 * DKT, T], F32)
    v_sb = place("v_sb", S2, [P, TT, D], F32)
    r_sb = place("r_sb", S2 + K16, [P, TT, D], F32)
    b_sb = place("b_sb", GU, [P, DKT, T], F32)
    la = place("la", GU + 8192, [P, TT, HK], F32)
    ex = place("ex", GU + 8192, [P, 2, DKT // 2, T], F32)
    q_t = place("q_t", S1, [P, MH, T], F32)
    k_t = place("k_t", S1 + K16, [P, MH, T], F32)
    o_hi = place("o_hi", S1, [P, MH, T], F32R)
    o_lo = place("o_lo", S1 + K16, [P, MH, T], F32R)
    mv_sb = place("mv_sb", S2, [P, TT, MH, P], F32)
    qr_t = place("qr_t", S2 + K16, [P, MH // 2, T], F32)
    cq_hi = place("cq_hi", S2 + K16 + 8192, [P, LT, T], F32R)
    cq_lo = place("cq_lo", S2 + K16 + 12288, [P, LT, T], F32R)
    ckv_hi = place("ckv_hi", GU, [P, LT, T], F32R)
    ckv_lo = place("ckv_lo", GU + 4096, [P, LT, T], F32R)
    y_out = place("y_out", S1, [P, TT, D], F32)

    cursor = [PR]

    def keep(name, shape, dt):
        n = 1
        for d in shape[1:]:
            n *= d
        n = (n * (1 if dt == I8 else 4) + 31) // 32 * 32
        t = place(name, cursor[0], shape, dt)
        cursor[0] += n
        return t

    ident = keep("ident", [P, P], F32)
    ones = keep("ones", [P, P], F32)
    tri = keep("tri", [P, P], F32)
    pcol = keep("pcol", [P, 3, P], F32)
    c_col = keep("c_col", [P, KT], F32)
    cv_col = keep("cv_col", [P, 2, 4, 2 * FT], F32)
    modc = keep("modc", [P, 2, KT], F32)
    ab = keep("ab", [P, 10, KT], F32)
    stats = keep("stats", [P, 3, 16], F32)
    half_neg = keep("half_neg", [P, 16], F32)
    pos_i = keep("pos_i", [P, TT], I32)
    pos_f = keep("pos_f", [P, TT], F32)
    inv = keep("inv", [P, HR], F32)
    cos = keep("cos", [P, TT, HR], F32)
    sin = keep("sin", [P, TT, HR], F32)
    TMP = cursor[0]
    limit = nc.sbuf_usable_end - base

    def tmp(name, offset, shape, dt):
        return place(name, TMP + offset, shape, dt)

    conv = tmp("conv", 0, [P, 2, 2, T], F32)
    gated = tmp("gated", 4096, [P, T], F32)
    both = tmp("both", 5120, [P, 2, T], F32)
    ang = tmp("ang", 7168, [P, 3, TT, HR], F32)
    st = tmp("st", 0, [P, HEADS, TT, P], F32)
    sx = tmp("sx", 4096, [P, HEADS, P], F32)
    mask = tmp("mask", 6144, [P, 8, P], I8)
    wg2 = tmp("wg2", 0, [RANK + 1, HK], F32)
    g1 = tmp("g1", 5120, [P, TT, RANK], F32)
    g1_t = tmp("g1_t", 4096, [32, T], F32)
    sc = tmp("sc", 0, [P, 3, P], F32)
    probs = tmp("probs", 1536, [P, 3, P], F32)
    p_t = tmp("p_t", 3072, [P, 3, P], F32)
    kr_t = tmp("kr_t", 4608, [P, T], F32)
    causal = tmp("causal", 5632, [P, 3, P], F32)
    rt = tmp("rt", 0, [P, 4, TT, 2, HR], F32)
    qr = tmp("qr", 2048, [P, TT, 2, ROPE], F32)
    kr = tmp("kr", 3072, [P, TT, 2, ROPE], F32)
    junk = place("junk", GU, [P, TT, W], F32)
    assert TMP + 7936 <= limit, (TMP + 7936, limit)

    MIX, FFN, KVN, HEAD, KVL, QL = 0, 32, 64, 80, 96, 100
    A_OF = {"mix0": 0, "ffn0": 2, "kv": 4, "mix1": 6, "ffn1": 8}

    def mod_source(g):
        if g in (6, 7):
            return kv_mod_w, (g - 6) * D
        layer, j = (0, g) if g < 6 else (1, g - 8)
        return mod_w[layer], j * D

    def mod_bias(g):
        if g in (6, 7):
            return 1, 96 + (g - 6) * KT
        return (1, g * KT) if g < 6 else (2, (g - 8) * KT)

    GATES = {2: 0, 5: 0, 10: 1, 13: 1}
    REDUCE = {0: ("pre", 0), 1: ("pre", 1), 2: ("mod_v", 0), 3: ("mod_v", 4), 4: ("mod_gla", 0),
              5: ("modu00", 0), 6: ("modd00", 0), 7: ("modu01", 0), 8: ("modd01", 0), 9: ("modd02", 0),
              10: ("mod_ukv", 0), 11: ("mod_uq", 0), 12: ("mod_mla", 0), 13: ("modu10", 0)}
    SHIFT = {0: ("mix0", MIX), 3: ("ffn0", FFN), 6: ("kv", KVN), 8: ("mix1", MIX + KT), 11: ("ffn1", FFN + KT)}
    SCALE = {1: ("mix0", MIX), 4: ("ffn0", FFN), 7: ("kv", KVN), 9: ("mix1", MIX + KT), 12: ("ffn1", FFN + KT)}

    def fills_of(g):
        return 4 if g in GATES else 1

    def reduce_at(g):
        name, k = REDUCE[g]
        return at[name].ms + k

    with ExitStack() as ctx:
        def sem(name):
            return ctx.enter_context(nc.semaphore(name))

        gm = ctx.enter_context(nc.psum_tensor("gm", [P, 2, TT, W], F32))
        tp = ctx.enter_context(nc.psum_tensor("tp", [P, 2, W], F32))
        ms = ctx.enter_context(nc.psum_tensor("ms", [P, 2, W], F32))

        raw_in = [sem(f"raw_in{i}") for i in range(RAW)]
        mod_in = [sem(f"mod_in{i}") for i in range(MODS)]
        rows_in = sem("rows_in")
        x_in = sem("x_in")
        gate_in = sem("gate_in")
        wg_in = sem("wg_in")
        out_in = sem("out_in")
        consts = sem("consts")
        hi_made = sem("hi_made")
        lo_made = sem("lo_made")
        item_used = sem("item_used")
        mod_used = sem("mod_used")
        acc_zero = sem("acc_zero")
        u_made = sem("u_made")
        tp_done = sem("tp_done")
        tp_free = sem("tp_free")
        ms_done = sem("ms_done")
        ms_free = sem("ms_free")
        x_added = sem("x_added")
        sums = sem("sums")
        rstd = sem("rstd")
        xn_made = sem("xn_made")
        split_hi = sem("split_hi")
        act_step = sem("act_step")
        dve_step = sem("dve_step")
        pool_step = sem("pool_step")
        c_act_made = sem("c_act_made")
        params = sem("params")
        columns_on = sem("columns_on")
        taps = sem("taps")
        conv_made = sem("conv_made")
        silu_made = sem("silu_made")
        gated_made = sem("gated_made")
        act_hi = sem("act_hi")
        act_lo = sem("act_lo")
        z_log = sem("z_log")
        e_made = sem("e_made")
        f_made = sem("f_made")
        xq_made = sem("xq_made")
        o_ready = sem("o_ready")
        o_sums = sem("o_sums")
        o_rstd = sem("o_rstd")
        o_gated = sem("o_gated")
        ang_made = sem("ang_made")
        sin_made = sem("sin_made")
        roped = sem("roped")
        s_made = sem("s_made")
        p_made = sem("p_made")
        p_norm = sem("p_norm")
        p_evac = sem("p_evac")
        o_split = sem("o_split")
        o_done = sem("o_done")

        block = ctx.enter_context(nc.Block())

        def halves(v, w, half):
            return v.rearrange("p t (g h r) -> p (t g) h r", h=2, r=w)[:, :, half, :]

        def head_fill(h, output):
            if output:
                k = 2 * h + 3 if h + 2 < MH else MH + h
            else:
                k = h if h < 2 else 2 * h - 2
            return at["heads"].ms + k

        LEVELS = [64, 32, 16, 8, 4, 2, 1]
        UNITS = [(P, 0), (P, 1)] + [(w, hh) for w in LEVELS for hh in (0, 1)]
        ffn_tiles = {}
        n = 0
        for layer in range(2):
            for g, blocks in enumerate(UP_BLOCKS):
                ffn_tiles[f"up{layer}{g}"] = n
                n += 4 * blocks
        added = {"gla_out": 0, "down00": 4, "down01": 8, "down02": 12, "mla_out": 16,
                 "down10": 20, "down11": 24, "down12": 28, "end": 32}
        NORM = {"norm0": 0, "norm1": 1, "norm2": 2, "norm3": 3, "norm4": 4, "norm5": 5, "final": 6}

        splits = {"norm0": 0, "o": 8, "norm1": 16, "norm2": 24, "norm3": 32, "norm4": 34, "norm5": 36}

        def made(fill):
            return fill + 1 - (fill > at["gate"].ms) - (fill > at["latent"].ms)

        @block.sync
        def _(sp):
            a = at

            def load_item(n, slot, src, words=ITEM, shape=KT_ITEM):
                if not (isinstance(n, int) and n < RAW):
                    sp.wait_ge(lo_made, n - RAW + 1)
                dst = raw[:, slot, 0:words].rearrange("p (j n) -> p j n", j=shape)
                sp.dma_start(dst, src).then_inc(raw_in[slot], 16)

            def load_mod(n, slot, g, kt):
                if not (isinstance(n, int) and n < MODS):
                    sp.wait_ge(mod_used, n - MODS + 1)
                w, col = mod_source(g)
                rows = w[kt * P:kt * P + P, :] if isinstance(kt, int) else w[bass.ds(kt * P, P), :]
                sp.dma_start(mods[:, slot, :], rows[:, col:col + D]).then_inc(mod_in[slot], 16)

            def columns(w, q, col, k_tiles=KT_ITEM, width=W):
                rows = w[q * k_tiles * P:(q + 1) * k_tiles * P, :]
                c = slice(col, col + width) if isinstance(col, int) else bass.ds(col, width)
                return rows[:, c].rearrange("(j p) n -> p j n", p=P)

            def product(name, group, mods_per, source):
                s = a[name]

                def body(i):
                    for k in range(8):
                        load_item(s.item + 8 * i + k, (s.item + k) % RAW, source(i, k // 4, k % 4))
                        mk = k - (8 - mods_per)
                        if mk >= 0:
                            load_mod(s.mod + mods_per * i + mk, mk % MODS, group, mods_per * i + mk)

                if s.item < RAW:
                    for i in range(s.n):
                        body(i)
                else:
                    with sp.Fori(0, s.n) as i:
                        body(i)

            for src, tile_, row in (
                (norm_mix_g, 0, MIX), (norm_ffn_g, 0, FFN), (kv_norm_g, 0, KVN),
                (gla_head_g, 0, HEAD), (mla_kv_norm_g, 0, KVL), (mla_q_norm_g, 0, QL),
                (mod_b[0], 1, 0), (kv_mod_b, 1, 96), (mod_b[1], 2, 0),
            ):
                names = "abcd"[:len(src.shape)]
                flat = src if len(names) == 1 else src.rearrange(" ".join(names) + " -> (" + " ".join(names) + ")")
                v = flat.rearrange("(r p) -> r p", p=P)
                sp.dma_start(prow[row:row + v.shape[0], tile_, :], v).then_inc(rows_in, 16)
            sp.dma_start(crow[:, 0, :], c.rearrange("o (r p) -> (o r) p", p=P)).then_inc(rows_in, 16)
            sp.dma_start(pos_i[:, :], positions.rearrange("o (t p) -> p (o t)", p=P),
                         allow_slow_non_contiguous=True).then_inc(rows_in, 16)
            for k in range(MODS):
                load_mod(k, k, 0, k)
            sp.dma_start(x_sb[:, :, :], x.rearrange("o (t p) d -> p (o t) d", p=P)).then_inc(x_in, 16)
            for layer in range(2):
                for k in range(3):
                    sp.dma_start(cvrow[:, 4 * layer + k, :],
                                 ffn_conv_w[layer, k].rearrange("(r p) -> r p", p=P)).then_inc(rows_in, 16)
                sp.dma_start(cvrow[:, 4 * layer + 3, :],
                             ffn_conv_b[layer].rearrange("(r p) -> r p", p=P)).then_inc(rows_in, 16)
            for k in range(MODS, 4):
                load_mod(k, k % MODS, 0, k)
            with sp.Fori(1, 4) as i:
                for k in range(4):
                    load_mod(4 * i + k, k % MODS, 0, 4 * i + k)
            with sp.Fori(0, 4) as i:
                for k in range(4):
                    load_mod(KT + 4 * i + k, k % MODS, 1, 4 * i + k)

            w_in = gla_w_in[0]
            s = a["gate"]
            g_src = w_in[:, 2 * HK + 2 * D:].rearrange("(j p) n -> p j n", p=P)
            load_item(s.item, s.item % RAW, g_src, KT * RANK, KT)
            sp.dma_start(wg2[0:RANK, :], gla_w_gate2[0]).then_inc(wg_in, 16)
            sp.dma_start(wg2[RANK:RANK + 1, :], gla_b_gate).then_inc(wg_in, 16)
            product("qk", 2, 8, lambda i, ch, q: columns(w_in, q, 1024 * i + W * ch))
            s = a["v"]
            for k in range(16):
                load_item(s.item + k, (s.item + k) % RAW, columns(w_in, k % 4, 2 * HK + W * (k // 4)))
                load_mod(s.mod + k, k % MODS, 3, k)
            product("r", None, 0, lambda i, ch, q: columns(w_in, q, 2 * HK + D + 1024 * i + W * ch))
            sp.wait_ge(ms_done, made(a["diag"].ms + 1))
            sp.wait_ge(xq_made, 2 * len(UNITS))
            sp.dma_start(x_sb[:, :, :], x.rearrange("o (t p) d -> p (o t) d", p=P)).then_inc(x_in, 16)
            product("gla_out", 4, 8, lambda i, ch, q: columns(gla_w_o[0], q, 1024 * i + W * ch))

            def ffn(layer, up_groups, down_groups, up_mods, down_mods):
                up, down = ffn_w_up[layer], ffn_w_down[layer]
                f0 = 0
                for g, blocks in enumerate(UP_BLOCKS):
                    product(f"up{layer}{g}", up_groups[g], up_mods[g],
                            lambda i, ch, q, f0=f0: columns(up, q, f0 + W * i + FF * ch))
                    name = f"down{layer}{g}"
                    s = a[name]
                    part = down[f0:f0 + blocks * W, :]
                    for k in range(16):
                        load_item(s.item + k, (s.item + k) % RAW,
                                  columns(part, k % 4, W * (k // 4), blocks), blocks * W, blocks)
                        if down_mods[g]:
                            load_mod(s.mod + k, k % MODS, down_groups[g], k)
                    f0 += blocks * W

            ffn(0, (5, 7, None), (6, 8, 9), (4, 4, 0), (8, 8, 8))

            s = a["latent"]
            for k in range(8):
                w = mla_w_dkv if k < 4 else mla_w_dq[0]
                load_item(s.item + k, (s.item + k) % RAW, columns(w, k % 4, 0))
            load_item(s.item + 8, (s.item + 8) % RAW,
                      mla_w_dkv[:, LAT:].rearrange("(j p) n -> p j n", p=P), KT * ROPE, KT)
            s = a["ukv"]
            for k in range(8):
                load_item(s.item + k, (s.item + k) % RAW, columns(mla_w_ukv, 0, W * k))
                for m in (2 * k, 2 * k + 1):
                    load_mod(s.mod + m, m % MODS, 10, m)
            s = a["uq"]
            for k in range(8):
                load_item(s.item + k, (s.item + k) % RAW, columns(mla_w_uq[0], 0, 384 * k, KT_ITEM, 384), 1536, 4)
                for m in (2 * k, 2 * k + 1):
                    load_mod(s.mod + m, m % MODS, 11, m)
            product("mla_out", 12, 8, lambda i, ch, q: columns(mla_w_o[0], q, 1024 * i + W * ch))
            ffn(1, (13, None, None), (None, None, None), (4, 0, 0), (0, 0, 0))

            sp.wait_ge(x_added, added["end"])
            sp.dma_start(gate_b[:, :], final_norm_g.partition_broadcast(P)).then_inc(gate_in, 16)
            o_v = out.rearrange("o (t p) d -> p (o t) d", p=P)
            for t in range(TT):
                sp.wait_ge(xn_made, 2 * NORM["final"] + t + 1)
                sp.dma_start(o_v[:, t, :], y_out[:, t, :]).then_inc(out_in, 16)
            sp.wait_ge(out_in, 16 * TT)

        @block.gpsimd
        def _(pool):
            step = Steps(pool, pool_step)
            step.mark(pool.memset(ident[:, :], 0.0))
            step.mark(pool.memset(ones[:, :], 1.0))
            step.mark(pool.memset(tri[:, :], 1.0))
            step.mark(pool.memset(half_neg[:, :], -0.5))
            step.mark(pool.memset(g1_t[:, :], 1.0))
            for k in range(HR):
                step.mark(pool.memset(inv[:, k:k + 1], float(10000.0 ** (-2.0 * k / ROPE))))
            step.wait(step.base + step.n)
            step.mark(pool.affine_select(out=ident[:, :], in_=ident[:, :], pattern=[[-1, P]],
                                         compare_op=ALU.not_equal, fill=1.0, base=0, channel_multiplier=1))
            pool.affine_select(out=tri[:, :], in_=tri[:, :], pattern=[[1, P]], compare_op=ALU.is_ge,
                               fill=0.0, base=0, channel_multiplier=-1).then_inc(consts, 1)
            for g in range(2):
                pool.memset(acc[:, g, :], 0.0).then_inc(acc_zero, 1)

            def clear(g):
                pool.wait_ge(ms_done, made(reduce_at(g - 2) + fills_of(g - 2) - 1))
                pool.memset(acc[:, g % 2, :], 0.0).then_inc(acc_zero, 1)

            def root(index, count, width, ready, ready_at, signal):
                pool.wait_ge(ready, ready_at)
                src, dst = stats[:, 0, index:index + count], stats[:, 1, index:index + count]
                step.link(pool.tensor_scalar(dst, src, 1.0 / width, EPS, ALU.mult, ALU.add))
                pool.tensor_tensor(dst, dst, half_neg[:, 0:count], ALU.pow).then_inc(signal, 1)

            def norm_root(name, width):
                root(TT * (NORM[name] % 2), TT, width, sums, TT * (NORM[name] + 1), rstd)

            norm_root("norm0", D)
            clear(2)
            pool.wait_ge(tp_free, at["norm0"].tp + 8)
            for k, w in enumerate(LEVELS):
                view = mask[:, k, :].rearrange("p (g h r) -> p g h r", h=2, r=w)[:, :, 1, :]
                step.link(pool.memset(mask[:, k, :], 0))
                step.link(pool.memset(view, 1))
                blocks = P // (2 * w)
                step.link(pool.affine_select(out=view, in_=view, pattern=[[-2 * w, blocks], [0, w]],
                                             compare_op=ALU.is_ge, fill=0.0, base=0, channel_multiplier=1))
                step.link(pool.affine_select(out=view, in_=view, pattern=[[2 * w, blocks], [0, w]],
                                             compare_op=ALU.is_ge, fill=0.0, base=w - 1, channel_multiplier=-1))
            step.link(pool.memset(mask[:, 7, :], 0))
            pool.affine_select(out=mask[:, 7, :], in_=mask[:, 7, :], pattern=[[-1, P]],
                               compare_op=ALU.not_equal, fill=1.0, base=0,
                               channel_multiplier=1).then_inc(consts, 1)
            clear(3)
            for n, (w, hh) in enumerate(UNITS):
                pool.wait_ge(f_made, n + 1)
                for half in range(2):
                    f, s = halves(ex[:, n % 2], w, half), halves(
                        qk_t[:, (0 if half else DKT) + 4 * hh:(0 if half else DKT) + 4 * hh + 4, :], w, half)
                    pool.tensor_tensor(f, f, s, ALU.mult).then_inc(xq_made, 1)
            clear(4)
            for h in range(HEADS):
                root(TT * h, TT, DV, o_sums, TT * (h + 1), o_rstd)
            norm_root("norm1", D)
            for g in range(5, 11):
                clear(g)
                if g == 10:
                    norm_root("norm2", D)
                    norm_root("norm3", LAT)
                    norm_root("norm4", LAT)
            pool.wait_ge(tp_free, at["norm4"].tp + 2)
            step.link(pool.memset(causal[:, :, :], 0.0))
            for k in (0, 2):
                ins = pool.affine_select(out=causal[:, k, :], in_=causal[:, k, :], pattern=[[-1, P]],
                                         compare_op=ALU.is_ge, fill=NEG, base=0, channel_multiplier=1)
                step.mark(ins) if k == 0 else ins.then_inc(consts, 1)
            clear(11)
            clear(12)
            clear(13)
            norm_root("norm5", D)
            norm_root("final", D)

        @block.scalar
        def _(act):
            a = at
            step = Steps(act, act_step)

            def hi(n, slot=None, words=ITEM):
                if isinstance(n, int) and n >= TOTAL:
                    return
                k = n if slot is None else slot
                act.wait_ge(raw_in[k % RAW], 16 * ((n - k % RAW) // RAW + 1) if isinstance(n, int)
                            else 4 * (n - k % RAW) + 16)
                if not (isinstance(n, int) and n < AHEAD):
                    act.wait_ge(item_used, n - AHEAD + 1)
                act.activation(w_hi[:, k % AHEAD, 0:words], raw[:, k % RAW, 0:words],
                               ACT.Copy).then_inc(hi_made, 1)

            def evac(last_item, par, dst, src=None, func=ACT.Copy):
                act.wait_ge(item_used, last_item + 1)
                act.activation(dst, gm[:, par] if src is None else src, func).then_inc(u_made, 1)

            def split(fill, count, dst, scale, shift):
                for f in range(count):
                    act.wait_ge(tp_done, fill + f + 1)
                    for k in range(2):
                        for d, sc_, sh_ in zip(dst, scale, shift):
                            kt = 2 * f + k
                            ins = act.activation(
                                d[:, kt, :], tp[:, (fill + f) % 2, k * T:(k + 1) * T], ACT.Identity,
                                scale=sc_[:, kt:kt + 1], bias=0.0 if sh_ is None else sh_[:, kt:kt + 1])
                    ins.then_inc(split_hi, 1)

            def squares(name, src, spare):
                for t in range(TT):
                    k = TT * (NORM[name] % 2) + t
                    act.activation(spare[:, t, :], src[:, t, :], ACT.Square,
                                   accum_out=stats[:, 0, k:k + 1]).then_inc(sums, 1)

            def load_gate(layer, part):
                act.dma_start(gate_b[:, :], mod_b[layer, part * D:(part + 1) * D].partition_broadcast(P))\
                   .then_inc(gate_in, 16)

            act.wait_ge(rows_in, 16 * 19)
            act.activation(crow[:, 1, :], crow[:, 0, :], ACT.Silu).then_inc(c_act_made, 1)
            act.wait_ge(ang_made, 1)
            act.activation(sin[:, :, :], ang[:, 0], ACT.Sin).then_inc(sin_made, 1)
            act.activation(cos[:, :, :], ang[:, 1], ACT.Sin).then_inc(sin_made, 1)
            act.wait_ge(x_in, 16)
            squares("norm0", x_sb, xn)
            act.wait_ge(columns_on, 1)
            split(a["norm0"].tp, 8, (h_hi,), (ab[:, A_OF["mix0"]],), (ab[:, A_OF["mix0"] + 1],))
            hi(0, words=KT * RANK)
            hi(1)
            hi(2)
            s = a["gate"]
            for f in range(4):
                t, half = f // 2, f % 2
                v = la[:, t, half * W:(half + 1) * W]
                act.wait_ge(ms_done, made(s.ms + 1 + f))
                step.link(act.activation(v, ms[:, (s.ms + 1 + f) % 2, :], ACT.Abs))
                step.link(act.activation(v, v, ACT.Exp, scale=-1.0))
                act.activation(v, v, ACT.Ln, bias=1.0).then_inc(z_log, 1)
            s = a["qk"]
            with act.Fori(0, s.n) as i:
                for k in range(8):
                    hi(s.item + AHEAD + 8 * i + k, s.item + AHEAD + k)
                    if k % 4 == 3:
                        par = k // 4
                        if par == 0:
                            act.wait_ge(ms_done, made(a["gate"].ms + 8))
                        act.wait_ge(tp_done, s.tp + 4 * i)
                        evac(s.item + 8 * i + k, par, u[:, par])
            s = a["v"]
            for k in range(16):
                hi(s.item + AHEAD + k)
                w, hh = UNITS[k]
                act.wait_ge(e_made, k + 1)
                act.activation(ex[:, k % 2], ex[:, k % 2], ACT.Exp, scale=1.0 / GATE_NORM).then_inc(f_made, 1)
                if k % 4 == 3:
                    ch = k // 4
                    evac(s.item + k, ch % 2, v_sb[:, :, ch * W:(ch + 1) * W])
            load_gate(0, 2)
            s = a["r"]
            with act.Fori(0, s.n) as i:
                for k in range(8):
                    hi(s.item + AHEAD + 8 * i + k, s.item + AHEAD + k)
                    if k % 4 == 3:
                        par = k // 4
                        evac(s.item + 8 * i + k, par, r_sb[:, :, bass.ds(1024 * i + par * W, W)],
                             func=ACT.Silu)
            for h in range(HEADS):
                act.wait_ge(o_ready, h + 1)
                for t in range(TT):
                    act.activation(ex[:, h % 2, 2 * t:2 * t + 2, :], gm[:, h % 2, t].rearrange("p (a b) -> p a b", a=2),
                                   ACT.Square, accum_out=stats[:, 0, TT * h + t:TT * h + t + 1])\
                       .then_inc(o_sums, 1)
            split(a["o"].tp, 8, (h_hi,), (pcol[:, 0, HEAD:HEAD + KT],), (None,))

            def add_section(name):
                s = a[name]

                def body(i):
                    for k in range(8):
                        hi(s.item + AHEAD + 8 * i + k, s.item + AHEAD + k)
                        if k % 4 == 3:
                            par = k // 4
                            if not (isinstance(i, int) and added[name] + 2 * i == 0):
                                act.wait_ge(x_added, added[name] + 2 * i)
                            evac(s.item + 8 * i + k, par, u[:, par])

                if added[name] == 0:
                    for i in range(s.n):
                        body(i)
                else:
                    with act.Fori(0, s.n) as i:
                        body(i)

            add_section("gla_out")
            act.wait_ge(x_added, added["down00"])
            squares("norm1", x_sb, xn)
            act.wait_ge(columns_on, 2)
            split(a["norm1"].tp, 8, (h_hi,), (ab[:, A_OF["ffn0"]],), (ab[:, A_OF["ffn0"] + 1],))

            def conv_tile(layer, g, blk, j, fill, tile_):
                s = a[f"up{layer}{g}"]
                bank = (s.tp + j) % 2
                ft = sum(UP_BLOCKS[:g]) * 4 + j
                act.wait_ge(tp_done, fill + 1)
                for side in range(2):
                    col = 4 * blk + (ft + side * FT)
                    cs = slice(col, col + 1) if isinstance(col, int) else bass.ds(col, 1)
                    ins = act.activation(conv[:, j % 2, side, :], tp[:, bank, side * T:(side + 1) * T],
                                         ACT.Identity, scale=cv_col[:, layer, 2, cs], bias=cv_col[:, layer, 3, cs])
                ins.then_inc(taps, 1)

            def conv_silu(j, tile_):
                act.wait_ge(conv_made, tile_ + 1)
                act.activation(conv[:, j % 2, 1, :], conv[:, j % 2, 1, :], ACT.Silu).then_inc(silu_made, 1)

            def conv_hi(blk, j, tile_):
                act.wait_ge(gated_made, tile_ + 1)
                kt = 4 * blk + j
                d = a_hi[:, kt, :] if isinstance(kt, int) else a_hi[:, bass.ds(kt, 1), :]
                s_ = gated[:, :] if isinstance(kt, int) else gated[:, :].rearrange("p (o t) -> p o t", o=1)
                act.activation(d, s_, ACT.Copy).then_inc(act_hi, 1)

            def up(layer, g):
                s = a[f"up{layer}{g}"]
                t0 = ffn_tiles[f"up{layer}{g}"]

                def body(i, conv_too):
                    for k in range(8):
                        if not conv_too and k == 3 and g > 0:
                            act.wait_ge(x_added, added[f"down{layer}{g - 1}"] + 4)
                        hi(s.item + AHEAD + 8 * i + k, s.item + AHEAD + k)
                        if conv_too and k < 4:
                            tile_ = t0 + 4 * (i - 1) + k
                            conv_tile(layer, g, i - 1, k, s.tp + 4 * (i - 1) + k, tile_)
                            conv_silu(k, tile_)
                            conv_hi(i - 1, k, tile_)
                        if k == 3:
                            if conv_too:
                                act.wait_ge(tp_done, s.tp + 4 * i)
                            evac(s.item + 8 * i + k, 0, u[:, 0])
                        if k == 7:
                            evac(s.item + 8 * i + k, 1, u[:, 1])

                body(0, False)
                if g == 0:
                    load_gate(layer, 5)
                with act.Fori(1, s.n) as i:
                    body(i, True)

            def last_tile(layer, g, k):
                s, n = a[f"up{layer}{g}"], UP_BLOCKS[g] - 1
                tile_ = ffn_tiles[f"up{layer}{g}"] + 4 * n + k
                conv_tile(layer, g, n, k, s.tp + 4 * n + k, tile_)
                conv_silu(k, tile_)
                conv_hi(n, k, tile_)

            def down(layer, g):
                name = f"down{layer}{g}"
                s = a[name]
                last_tile(layer, g, 0)
                last_tile(layer, g, 1)
                for k in range(16):
                    hi(s.item + AHEAD + k)
                    if k < 2:
                        last_tile(layer, g, k + 2)
                    if k % 4 == 3:
                        ch = k // 4
                        if ch >= 2:
                            act.wait_ge(x_added, added[name] + ch - 1)
                        evac(s.item + k, ch % 2, u[:, ch % 2])

            for g in range(3):
                up(0, g)
                down(0, g)
            act.wait_ge(x_added, added["mla_out"])
            squares("norm2", x_sb, xn)
            act.wait_ge(columns_on, 4)
            split(a["norm2"].tp, 8, (h_hi, a_hi), (ab[:, A_OF["mix1"]], ab[:, A_OF["kv"]]),
                  (ab[:, A_OF["mix1"] + 1], ab[:, A_OF["kv"] + 1]))
            s = a["latent"]
            for k in range(9):
                hi(s.item + AHEAD + k)
                if k in (3, 7):
                    evac(s.item + k, k // 4, u[:, k // 4])
                    act.wait_ge(u_made, s.chunk + k // 4 + 1)
                    squares("norm3" if k == 3 else "norm4", u[:, k // 4], junk)
            split(a["norm3"].tp, 2, (ckv_hi,), (pcol[:, 0, KVL:KVL + LT],), (None,))
            split(a["norm4"].tp, 2, (cq_hi,), (pcol[:, 0, QL:QL + LT],), (None,))
            s = a["ukv"]
            for k in range(8):
                hi(s.item + AHEAD + k)
                act.wait_ge(item_used, s.item + k + 1)
                if k >= 2:
                    act.wait_ge(tp_done, s.tp + k - 1)
                else:
                    act.wait_ge(tp_done, a["norm4"].tp + 2)
                src = gm[:, k % 2].rearrange("p t (h v n) -> p t h v n", h=2, v=2)
                act.activation(u[:, k % 2, :, 0:2 * P].rearrange("p t (h n) -> p t h n", h=2),
                               src[:, :, :, 0, :], ACT.Copy)
                act.activation(mv_sb[:, :, 2 * k:2 * k + 2, :], src[:, :, :, 1, :], ACT.Copy).then_inc(u_made, 1)
            load_gate(1, 2)
            s = a["uq"]
            for k in range(8):
                hi(s.item + AHEAD + k)
                act.wait_ge(tp_done, s.tp + 2 * (k - 1) if k >= 2 else a["ukv"].tp + 8)
                evac(s.item + k, k % 2, u[:, k % 2, :, 0:384], src=gm[:, k % 2, :, 0:384])
            f = a["heads"].ms
            for h in range(MH + 2):
                if h < MH:
                    act.wait_ge(s_made, h + 1)
                    for b, (c0, c1) in enumerate(((0, 1), (1, 3))):
                        if h >= 1:
                            act.wait_ge(tp_done, a["heads"].tp + h)
                        k = 4 * (h % 2) + b
                        act.activation(probs[:, c0:c1, :], sc[:, c0:c1, :], ACT.Exp, scale=MSCALE,
                                       bias=stats[:, 2, k:k + 1],
                                       accum_out=stats[:, 2, k + 2:k + 3]).then_inc(p_made, 1)
                if h >= 2:
                    act.wait_ge(ms_done, made(head_fill(h - 2, True)))
                    act.activation(o_hi[:, h - 2, :], ms[:, head_fill(h - 2, True) % 2, 0:T],
                                   ACT.Copy).then_inc(o_split, 1)
            add_section("mla_out")
            act.wait_ge(x_added, added["down10"])
            squares("norm5", x_sb, xn)
            act.wait_ge(columns_on, 5)
            split(a["norm5"].tp, 8, (h_hi,), (ab[:, A_OF["ffn1"]],), (ab[:, A_OF["ffn1"] + 1],))
            for g in range(3):
                up(1, g)
                down(1, g)
            act.wait_ge(x_added, added["end"])
            squares("final", x_sb, y_out)

        @block.vector
        def _(dve):
            a = at
            step = Steps(dve, dve_step)

            def lo(n, slot=None, words=ITEM):
                if isinstance(n, int) and n >= TOTAL:
                    return
                k = n if slot is None else slot
                dve.wait_ge(hi_made, n + 1)
                dve.tensor_tensor(w_lo[:, k % AHEAD, 0:words], raw[:, k % RAW, 0:words],
                                  w_hi[:, k % AHEAD, 0:words].bitcast(F32), ALU.subtract).then_inc(lo_made, 1)

            def mod(n, slot, g, kt):
                if isinstance(n, int):
                    dve.wait_ge(mod_in[slot], 16 * (n // MODS + 1))
                    if n:
                        dve.wait_ge(mod_used, n)
                else:
                    dve.wait_ge(mod_in[slot], 8 * (n - slot) + 16)
                    dve.wait_ge(mod_used, n)
                ck = c_col[:, kt:kt + 1] if isinstance(kt, int) else c_col[:, bass.ds(kt, 1)]
                dve.scalar_tensor_tensor(acc[:, g % 2, :], mods[:, slot, :], ck, acc[:, g % 2, :],
                                         ALU.mult, ALU.add).then_inc(mod_used, 1)

            def reduced(g):
                fill = reduce_at(g)
                if g in GATES:
                    dve.wait_ge(gate_in, 16 * (list(GATES).index(g) + 1))
                    for j in range(4):
                        dve.wait_ge(ms_done, made(fill + j))
                        v = gate_b[:, j * W:(j + 1) * W]
                        dve.scalar_tensor_tensor(v, ms[:, (fill + j) % 2, :], 1.0, v,
                                                 ALU.add, ALU.add).then_inc(ms_free, 1)
                    dve.wait_ge(ms_free, fill + 4)
                else:
                    tile_, col = mod_bias(g)
                    bias = pcol[:, tile_, col:col + KT]
                    dve.wait_ge(ms_done, made(fill))
                    psum = ms[:, fill % 2, 0:KT]
                    if g in SHIFT:
                        dve.tensor_tensor(ab[:, A_OF[SHIFT[g][0]] + 1, :], psum, bias, ALU.add).then_inc(ms_free, 1)
                        dve.wait_ge(ms_free, fill + 1)
                    else:
                        norm, gain = SCALE[g]
                        dve.tensor_tensor(modc[:, 0, :], psum, bias, ALU.add).then_inc(ms_free, 1)
                        dve.wait_ge(ms_free, fill + 1)
                        dve.scalar_tensor_tensor(ab[:, A_OF[norm], :], modc[:, 0, :], 1.0,
                                                 pcol[:, 0, gain:gain + KT], ALU.add,
                                                 ALU.mult).then_inc(columns_on, 1)
                        dve.wait_ge(columns_on, list(SCALE).index(g) + 1)

            def split(name, count, dst, hi_of, scale, shift):
                fill = a[name].tp
                for f in range(count):
                    dve.wait_ge(split_hi, splits[name] + f + 1)
                    for m, (d, h_, sc_, sh_) in enumerate(zip(dst, hi_of, scale, shift)):
                        for k in range(2):
                            kt = 2 * f + k
                            t = tp[:, (fill + f) % 2, k * T:(k + 1) * T]
                            if sh_ is None:
                                ins = dve.tensor_scalar(both[:, k, :], t, sc_[:, kt:kt + 1], None, ALU.mult)
                            else:
                                ins = dve.tensor_scalar(both[:, k, :], t, sc_[:, kt:kt + 1], sh_[:, kt:kt + 1],
                                                        ALU.mult, ALU.add)
                            v = step.mark(ins)
                        step.wait(v)
                        ins = dve.tensor_tensor(d[:, 2 * f:2 * f + 2, :], both[:, :, :],
                                                h_[:, 2 * f:2 * f + 2, :].bitcast(F32), ALU.subtract)
                        if m == len(dst) - 1:
                            ins.then_inc(tp_free, 1)
                        else:
                            step.link(ins)
                    dve.wait_ge(tp_free, fill + f + 1)

            def normalised(name, src, dst):
                dve.wait_ge(rstd, NORM[name] + 1)
                for t in range(TT):
                    k = TT * (NORM[name] % 2) + t
                    dve.tensor_scalar(dst[:, t, :], src[:, t, :], stats[:, 1, k:k + 1], None,
                                      ALU.mult).then_inc(xn_made, 1)

            def add_chunk(chunk, par, cols):
                dve.wait_ge(u_made, chunk + 1)
                g = gate_b[:, cols].rearrange("p (o n) -> p o n", o=1).to_broadcast([P, TT, W])
                step.link(dve.tensor_tensor(u[:, par], u[:, par], g, ALU.mult))
                dve.tensor_tensor(x_sb[:, :, cols], x_sb[:, :, cols], u[:, par], ALU.add).then_inc(x_added, 1)

            def section(name, group, mods_per, extra=None):
                s = a[name]
                if mods_per:
                    dve.wait_ge(acc_zero, group + 1)
                links = {None: 0, "add": 2}[extra]
                with dve.Fori(0, s.n) as i, step.loop(i, 0, s.n, links):
                    for k in range(8):
                        mk = k - (8 - mods_per)
                        if mk >= 0:
                            mod(s.mod + mods_per * i + mk, mk % MODS, group, mods_per * i + mk)
                        lo(s.item + AHEAD + 8 * i + k, s.item + AHEAD + k)
                        if extra == "add" and k % 4 == 3:
                            par = k // 4
                            add_chunk(s.chunk + 2 * i + par, par, bass.ds(1024 * i + par * W, W))

            def evac_tp(fill, dst, src, scale=None):
                dve.wait_ge(tp_done, fill + 1)
                if scale is None:
                    dve.tensor_copy(dst, src).then_inc(tp_free, 1)
                else:
                    dve.tensor_scalar(dst, src, scale, None, ALU.mult).then_inc(tp_free, 1)

            dve.wait_ge(consts, 1)
            dve.wait_ge(rows_in, 16 * 19)
            step.link(dve.tensor_copy(pos_f[:, :], pos_i[:, :]))
            for t in range(TT):
                step.link(dve.tensor_scalar(ang[:, 2, t, :], inv[:, :], pos_f[:, t:t + 1], None, ALU.mult))
            step.link(dve.tensor_scalar(ang[:, 1], ang[:, 2], 1.0 / TWO_PI, ROUND, ALU.mult, ALU.add))
            step.link(dve.tensor_scalar(ang[:, 1], ang[:, 1], -ROUND, None, ALU.add))
            for part in (*SPLIT_2PI, TWO_PI - sum(SPLIT_2PI)):
                step.link(dve.scalar_tensor_tensor(ang[:, 2], ang[:, 1], -part, ang[:, 2], ALU.mult, ALU.add))
            step.link(dve.tensor_scalar(ang[:, 0], ang[:, 2], 3.1415925, -3.1415925, ALU.min, ALU.max))
            dve.tensor_scalar(ang[:, 1], ang[:, 0], 0.5, None, ALU.mult).then_inc(ang_made, 1)
            s = a["setup"]
            dve.wait_ge(tp_done, 1)
            for t, rows in enumerate((104, P, 96)):
                step.mark(dve.tensor_copy(pcol[:, t, 0:rows], tp[:, 0, t * P:t * P + rows]))
            dve.tensor_copy(c_col[:, :], tp[:, 0, 3 * P:3 * P + KT]).then_inc(tp_free, 1)
            for layer in range(2):
                evac_tp(1 + layer, cv_col[:, layer], tp[:, (1 + layer) % 2, 0:8 * FT].rearrange("p (k c) -> p k c", k=4))
            dve.wait_ge(tp_free, 3)
            dve.wait_ge(sin_made, 2)
            step.link(dve.tensor_tensor(cos[:, :, :], cos[:, :, :], cos[:, :, :], ALU.mult))
            step.link(dve.tensor_scalar(cos[:, :, :], cos[:, :, :], -2.0, 1.0, ALU.mult, ALU.add))
            dve.wait_ge(acc_zero, 2)
            for k in range(4):
                mod(k, k % MODS, 0, k)
            with dve.Fori(1, 4) as i:
                for k in range(4):
                    mod(4 * i + k, k % MODS, 0, 4 * i + k)
            normalised("norm0", x_sb, xn)
            with dve.Fori(0, 4) as i:
                for k in range(4):
                    mod(KT + 4 * i + k, k % MODS, 1, 4 * i + k)
            reduced(0)
            reduced(1)
            split("norm0", 8, (h_lo,), (h_hi,), (ab[:, A_OF["mix0"]],), (ab[:, A_OF["mix0"] + 1],))
            lo(0, words=KT * RANK)
            lo(1)
            s = a["gate"]
            dve.wait_ge(item_used, s.item + 1)
            dve.tensor_copy(g1[:, :, :], ms[:, s.ms % 2, 0:TT * RANK].rearrange("p (t r) -> p t r", t=TT))\
               .then_inc(ms_free, 1)
            evac_tp(s.tp, g1_t[0:RANK, :], tp[0:RANK, s.tp % 2, 0:T])
            lo(2)
            for f in range(4):
                t, half = f // 2, f % 2
                v = la[:, t, half * W:(half + 1) * W]
                dve.wait_ge(z_log, f + 1)
                dve.scalar_tensor_tensor(v, ms[:, (s.ms + 1 + f) % 2, :], 0.0, v, ALU.min,
                                         ALU.subtract).then_inc(ms_free, 1)
            for f in range(4):
                t, half = f // 2, f % 2
                dve.wait_ge(ms_done, made(s.ms + 5 + f))
                dve.tensor_copy(b_sb[:, 4 * half:4 * half + 4, t * P:(t + 1) * P],
                                ms[:, (s.ms + 5 + f) % 2, :].rearrange("p (k i) -> p k i", k=4)).then_inc(ms_free, 1)
            s = a["qk"]
            dve.wait_ge(acc_zero, 3)

            def turned(fill, j, i):
                tile_ = DKT * i + 2 * j
                dst = qk_t[:, tile_:tile_ + 2, :] if isinstance(tile_, int) else qk_t[:, bass.ds(tile_, 2), :]
                evac_tp(fill, dst, tp[:, (s.tp + j) % 2, :].rearrange("p (k t) -> p k t", k=2), 0.25)

            def qk_body(i, turn):
                for k in range(8):
                    mod(s.mod + 8 * i + k, k % MODS, 2, 8 * i + k)
                    lo(s.item + AHEAD + 8 * i + k, s.item + AHEAD + k)
                    if turn and k < 4:
                        turned(s.tp + 4 * (i - 1) + k, k, i - 1)

            qk_body(0, False)
            qk_body(1, True)
            for k in range(4):
                turned(s.tp + 4 + k, k, 1)
            s = a["diag"]
            step.link(dve.memset(st[:, :, :, :], 0.0))
            dve.wait_ge(consts, 2)

            def pick(fill, level, hh):
                dve.wait_ge(ms_done, made(fill))
                dve.copy_predicated(
                    st[:, 2 * hh:2 * hh + 2, :, :].rearrange("p h t i -> p (h t) i"),
                    mask[:, level:level + 1, :].to_broadcast([P, 4, P]),
                    ms[:, fill % 2, :].rearrange("p (k i) -> p k i", k=4)).then_inc(ms_free, 1)

            for hh in range(2):
                pick(s.ms + hh, 7, hh)

            def exponents(n):
                w, hh = UNITS[n]
                b = b_sb[:, 4 * hh:4 * hh + 4, :]
                first, second = halves(b, w, 0), halves(b, w, 1)
                middle = first[:, :, w - 1:w].to_broadcast([P, 4 * T // (2 * w), w])
                if n >= 2:
                    dve.wait_ge(ms_done, made(a["v"].ms + n - 2))
                step.mark(dve.tensor_tensor(halves(ex[:, n % 2], w, 0), middle, first, ALU.subtract))
                if w == P:
                    dve.tensor_copy(halves(ex[:, n % 2], w, 1), second).then_inc(e_made, 1)
                else:
                    dve.tensor_tensor(halves(ex[:, n % 2], w, 1), second, middle, ALU.subtract).then_inc(e_made, 1)

            def picked(n):
                w, hh = UNITS[n]
                fill = a["v"].ms + n
                if w == P:
                    dve.wait_ge(ms_done, made(fill))
                    dve.tensor_copy(sx[:, 2 * hh:2 * hh + 2, :],
                                    ms[:, fill % 2, 0:2 * P].rearrange("p (h i) -> p h i", h=2)).then_inc(ms_free, 1)
                else:
                    pick(fill, LEVELS.index(w), hh)

            s = a["v"]
            dve.wait_ge(ms_free, a["gate"].ms + 9)
            dve.wait_ge(acc_zero, 4)
            for k in range(16):
                exponents(k)
                mod(s.mod + k, k % MODS, 3, k)
                lo(s.item + AHEAD + k)
                if k:
                    dve.wait_ge(ms_free, s.ms + k - 1)
                    picked(k - 1)
            dve.wait_ge(ms_free, s.ms + 15)
            picked(15)
            reduced(2)
            reduced(3)
            section("r", None, 0)
            for h in range(HEADS):
                dve.wait_ge(o_rstd, h + 1)
                for t in range(TT):
                    v = r_sb[:, t, h * DV:(h + 1) * DV]
                    ins = dve.scalar_tensor_tensor(v, gm[:, h % 2, t, :], stats[:, 1, TT * h + t:TT * h + t + 1],
                                                   v, ALU.mult, ALU.mult)
                    step.mark(ins) if t == 0 else ins.then_inc(o_gated, 1)
            split("o", 8, (h_lo,), (h_hi,), (pcol[:, 0, HEAD:HEAD + KT],), (None,))
            dve.wait_ge(x_in, 32)
            section("gla_out", 4, 8, "add")
            reduced(4)
            dve.wait_ge(x_added, 4)
            normalised("norm1", x_sb, xn)
            split("norm1", 8, (h_lo,), (h_hi,), (ab[:, A_OF["ffn0"]],), (ab[:, A_OF["ffn0"] + 1],))

            def conv_tile(layer, g, blk, j, fill, tile_):
                bank = (a[f"up{layer}{g}"].tp + j) % 2
                ft = sum(UP_BLOCKS[:g]) * 4 + j
                dve.wait_ge(taps, tile_ + 1)
                for tap, shift in ((1, 1), (0, 2)):
                    for side in (1, 0):
                        col = 4 * blk + (ft + side * FT)
                        cs = slice(col, col + 1) if isinstance(col, int) else bass.ds(col, 1)
                        v = conv[:, j % 2, side, shift:T]
                        ins = dve.scalar_tensor_tensor(v, tp[:, bank, side * T:(side + 1) * T - shift],
                                                       cv_col[:, layer, tap, cs], v, ALU.mult, ALU.add)
                        if tap:
                            last = step.mark(ins)
                        elif side:
                            ins.then_inc(conv_made, 1)
                        else:
                            ins.then_inc(tp_free, 1)
                    if tap:
                        step.wait(last)
                dve.wait_ge(silu_made, tile_ + 1)
                dve.wait_ge(tp_free, fill + 1)
                dve.tensor_tensor(gated[:, :], conv[:, j % 2, 0, :], conv[:, j % 2, 1, :],
                                  ALU.mult).then_inc(gated_made, 1)
                dve.wait_ge(act_hi, tile_ + 1)
                kt = 4 * blk + j
                ks = slice(kt, kt + 1) if isinstance(kt, int) else bass.ds(kt, 1)
                dve.tensor_tensor(a_lo[:, ks, :], gated[:, :].rearrange("p (o t) -> p o t", o=1),
                                  a_hi[:, ks, :].bitcast(F32), ALU.subtract).then_inc(act_lo, 1)

            def up(layer, g, group, mods_per):
                s = a[f"up{layer}{g}"]
                t0 = ffn_tiles[f"up{layer}{g}"]
                if mods_per:
                    dve.wait_ge(acc_zero, group + 1)

                def body(i, conv_too):
                    for k in range(8):
                        mk = k - (8 - mods_per)
                        if mk >= 0:
                            mod(s.mod + mods_per * i + mk, mk % MODS, group, mods_per * i + mk)
                        lo(s.item + AHEAD + 8 * i + k, s.item + AHEAD + k)
                        if conv_too and k < 4:
                            conv_tile(layer, g, i - 1, k, s.tp + 4 * (i - 1) + k, t0 + 4 * (i - 1) + k)

                body(0, False)
                with dve.Fori(1, s.n) as i, step.loop(i, 1, s.n, 8):
                    body(i, True)

            def last_tile(layer, g, k):
                s, n = a[f"up{layer}{g}"], UP_BLOCKS[g] - 1
                conv_tile(layer, g, n, k, s.tp + 4 * n + k, ffn_tiles[f"up{layer}{g}"] + 4 * n + k)

            def down(layer, g, up_group, group):
                s = a[f"down{layer}{g}"]
                last_tile(layer, g, 0)
                last_tile(layer, g, 1)
                if up_group is not None:
                    reduced(up_group)
                if group is not None:
                    dve.wait_ge(acc_zero, group + 1)
                for k in range(16):
                    if group is not None:
                        mod(s.mod + k, k % MODS, group, k)
                    lo(s.item + AHEAD + k)
                    if k < 2:
                        last_tile(layer, g, k + 2)
                    if k % 4 == 3:
                        ch = k // 4
                        add_chunk(s.chunk + ch, ch % 2, slice(ch * W, (ch + 1) * W))
                if group is not None:
                    reduced(group)

            for g, (ug, um, dg) in enumerate(((5, 4, 6), (7, 4, 8), (None, 0, 9))):
                up(0, g, ug, um)
                down(0, g, ug, dg)

            dve.wait_ge(x_added, added["mla_out"])
            normalised("norm2", x_sb, xn)
            split("norm2", 8, (h_lo, a_lo), (h_hi, a_hi), (ab[:, A_OF["mix1"]], ab[:, A_OF["kv"]]),
                  (ab[:, A_OF["mix1"] + 1], ab[:, A_OF["kv"] + 1]))
            s = a["latent"]
            for k in range(9):
                lo(s.item + AHEAD + k)

            def rotate(x1, x2, out1, out2, n):
                cb = cos[:, :, :].rearrange("p t (o r) -> p t o r", o=1).to_broadcast([P, TT, n, HR])
                sb_ = sin[:, :, :].rearrange("p t (o r) -> p t o r", o=1).to_broadcast([P, TT, n, HR])
                for k, (v, w_) in enumerate(((x1, cb), (x2, sb_), (x2, cb), (x1, sb_))):
                    last = step.mark(dve.tensor_tensor(rt[:, k, :, 0:n, :], v, w_, ALU.mult))
                step.wait(last)
                step.mark(dve.tensor_tensor(out1, rt[:, 0, :, 0:n, :], rt[:, 1, :, 0:n, :], ALU.subtract))
                return dve.tensor_tensor(out2, rt[:, 2, :, 0:n, :], rt[:, 3, :, 0:n, :], ALU.add)

            normalised("norm3", u[:, 0], u[:, 0])
            normalised("norm4", u[:, 1], u[:, 1])
            dve.wait_ge(item_used, s.item + 9)
            kv = ms[:, s.ms % 2, 0:TT * ROPE].rearrange("p (t o r) -> p t o r", t=TT, o=1)
            ins = rotate(kv[:, :, :, 0:HR], kv[:, :, :, HR:ROPE], kr[:, :, 0:1, 0:HR], kr[:, :, 0:1, HR:ROPE], 1)
            ins.then_inc(ms_free, 1)
            dve.wait_ge(ms_free, s.ms + 1)
            dve.tensor_copy(kr[:, :, 1, :], kr[:, :, 0, :]).then_inc(roped, 1)
            split("norm3", 2, (ckv_lo,), (ckv_hi,), (pcol[:, 0, KVL:KVL + LT],), (None,))
            split("norm4", 2, (cq_lo,), (cq_hi,), (pcol[:, 0, QL:QL + LT],), (None,))
            evac_tp(a["krope"].tp, kr_t[:, :], tp[:, a["krope"].tp % 2, 0:T])

            s = a["ukv"]
            dve.wait_ge(acc_zero, 11)

            def keys(k):
                evac_tp(s.tp + k, k_t[:, 2 * k:2 * k + 2, :],
                        tp[:, (s.tp + k) % 2, :].rearrange("p (h t) -> p h t", h=2))

            for k in range(8):
                for m in (2 * k, 2 * k + 1):
                    mod(s.mod + m, m % MODS, 10, m)
                lo(s.item + AHEAD + k)
                if k:
                    keys(k - 1)
            keys(7)
            reduced(10)
            q = a["uq"]
            dve.wait_ge(acc_zero, 12)

            def queries(k):
                f = q.tp + 2 * k
                evac_tp(f, q_t[:, 2 * k:2 * k + 2, :], tp[:, f % 2, :].rearrange("p (h t) -> p h t", h=2))
                evac_tp(f + 1, qr_t[:, k, :], tp[:, (f + 1) % 2, 0:T])

            for k in range(8):
                for m in (2 * k, 2 * k + 1):
                    mod(q.mod + m, m % MODS, 11, m)
                lo(q.item + AHEAD + k)
                if k:
                    queries(k - 1)
                dve.wait_ge(u_made, q.chunk + k + 1)
                v = u[:, k % 2, :, 0:384].rearrange("p t (h c) -> p t h c", h=2)
                rotate(v[:, :, :, P:P + HR], v[:, :, :, P + HR:P + ROPE],
                       qr[:, :, :, 0:HR], qr[:, :, :, HR:ROPE], 2).then_inc(roped, 1)
            queries(7)
            reduced(11)
            f = a["heads"]
            dve.wait_ge(consts, 3)
            for h in range(MH + 2):
                if 1 <= h <= MH:
                    k = 4 * ((h - 1) % 2)
                    dve.wait_ge(p_made, 2 * h)
                    step.link(dve.reciprocal(stats[:, 2, 8:10], stats[:, 2, k + 2:k + 4]))
                    step.mark(dve.tensor_scalar(probs[:, 0, :], probs[:, 0, :], stats[:, 2, 8:9], None, ALU.mult))
                    dve.tensor_scalar(probs[:, 1:3, :], probs[:, 1:3, :], stats[:, 2, 9:10], None,
                                      ALU.mult).then_inc(p_norm, 1)
                if h < MH:
                    fill = head_fill(h, False)
                    dve.wait_ge(ms_done, made(fill))
                    dve.tensor_tensor(sc[:, :, :], ms[:, fill % 2, 0:3 * P].rearrange("p (b k) -> p b k", b=3),
                                      causal[:, :, :], ALU.add).then_inc(ms_free, 1)
                    dve.wait_ge(ms_free, fill + 1)
                    step.mark(dve.reduce_max(stats[:, 2, 10:11], sc[:, 0, :], AX_X))
                    step.link(dve.reduce_max(stats[:, 2, 11:12], sc[:, 1:3, :].rearrange("p a b -> p (a b)"), AX_X))
                    k = 4 * (h % 2)
                    dve.tensor_scalar(stats[:, 2, k:k + 2], stats[:, 2, 10:12], -MSCALE, None,
                                      ALU.mult).then_inc(s_made, 1)
                if 1 <= h <= MH:
                    t = f.tp + h - 1
                    dve.wait_ge(tp_done, t + 1)
                    if h >= 2:
                        dve.wait_ge(ms_done, made(head_fill(h - 2, True)))
                    dve.tensor_copy(p_t[:, :, :], tp[:, t % 2, 0:3 * P].rearrange("p (b k) -> p b k", b=3))\
                       .then_inc(tp_free, 1)
                if h >= 2:
                    fill = head_fill(h - 2, True)
                    dve.wait_ge(o_split, h - 1)
                    dve.tensor_tensor(o_lo[:, h - 2, :], ms[:, fill % 2, 0:T], o_hi[:, h - 2, :].bitcast(F32),
                                      ALU.subtract).then_inc(ms_free, 1)
            section("mla_out", 12, 8, "add")
            reduced(12)
            dve.wait_ge(x_added, added["down10"])
            normalised("norm5", x_sb, xn)
            split("norm5", 8, (h_lo,), (h_hi,), (ab[:, A_OF["ffn1"]],), (ab[:, A_OF["ffn1"] + 1],))
            for g in range(3):
                up(1, g, 13 if g == 0 else None, 4 if g == 0 else 0)
                down(1, g, 13 if g == 0 else None, None)
            dve.wait_ge(gate_in, 16 * 5)
            dve.wait_ge(rstd, NORM["final"] + 1)
            for t in range(TT):
                k = TT * (NORM["final"] % 2) + t
                dve.scalar_tensor_tensor(y_out[:, t, :], x_sb[:, t, :], stats[:, 1, k:k + 1], gate_b[:, :],
                                         ALU.mult, ALU.mult).then_inc(xn_made, 1)

        @block.tensor
        def _(pe):
            a = at

            def item(n, slot, hi_s, lo_s, par, q, k_tiles=KT_ITEM, width=W, total=KT):
                pe.wait_ge(lo_made, n + 1)
                wh = w_hi[:, slot % AHEAD, 0:k_tiles * width].rearrange("p (j n) -> p j n", j=k_tiles)
                wl = w_lo[:, slot % AHEAD, 0:k_tiles * width].rearrange("p (j n) -> p j n", j=k_tiles)
                for j in range(k_tiles):
                    kt = q * k_tiles + j
                    for t in range(TT):
                        o, tok = gm[:, par, t, 0:width], slice(t * P, (t + 1) * P)
                        pe.matmul(o, hi_s[:, kt, tok], wh[:, j, :], start=kt == 0, stop=False)
                        pe.matmul(o, hi_s[:, kt, tok], wl[:, j, :], start=False, stop=False)
                        ins = pe.matmul(o, lo_s[:, kt, tok], wh[:, j, :], start=False, stop=kt == total - 1)
                ins.then_inc(item_used, 1)

            def gm_free(chunk):
                if not (isinstance(chunk, int) and chunk < 2):
                    pe.wait_ge(u_made, chunk - 1)

            def transposes(fill, bank, parts):
                if not (isinstance(fill, int) and fill < 2):
                    pe.wait_ge(tp_free, fill - 1)
                for src, col in parts:
                    k, m = src.shape[0], src.shape[1]
                    ins = pe.transpose(tp[0:m, bank, col:col + k], src, ident[0:k, 0:k])
                ins.then_inc(tp_done, 1)

            def ms_open(fill):
                if fill >= 2:
                    pe.wait_ge(ms_free, fill - 1)
                return ms[:, fill % 2, :]

            def narrow(n, fill, hi_s, lo_s, width):
                pe.wait_ge(lo_made, n + 1)
                o = ms_open(fill)
                wh = w_hi[:, n % AHEAD, 0:KT * width].rearrange("p (j n) -> p j n", j=KT)
                wl = w_lo[:, n % AHEAD, 0:KT * width].rearrange("p (j n) -> p j n", j=KT)
                for t in range(TT):
                    v, tok = o[:, t * width:(t + 1) * width], slice(t * P, (t + 1) * P)
                    for kt in range(KT):
                        pe.matmul(v, hi_s[:, kt, tok], wh[:, kt, :], start=kt == 0, stop=False)
                        pe.matmul(v, hi_s[:, kt, tok], wl[:, kt, :], start=False, stop=False)
                        ins = pe.matmul(v, lo_s[:, kt, tok], wh[:, kt, :], start=False, stop=kt == KT - 1)
                ins.then_inc(item_used, 1)

            def reduce_mod(g):
                name = REDUCE[g][0]
                pe.wait_ge(mod_used, KT * (g + 1))
                fill = reduce_at(g)
                if g in GATES:
                    for j in range(4):
                        o = ms_open(fill + j)
                        pe.matmul(o, ones[:, :], acc[:, g % 2, j * W:(j + 1) * W],
                                  start=True, stop=True).then_inc(ms_done, 1)
                else:
                    o = ms_open(fill)
                    for j in range(KT):
                        ins = pe.matmul(o[:, j:j + 1], acc[:, g % 2, j * P:(j + 1) * P], ones[:, 0:1],
                                        start=True, stop=True)
                    ins.then_inc(ms_done, 1)

            def turn_rows(name, count, tile_of):
                s = a[name]
                for f in range(count):
                    transposes(s.tp + f, (s.tp + f) % 2,
                               [(tile_of(2 * f + k, t), k * T + t * P) for k in range(2) for t in range(TT)])

            def turn_norm(name):
                pe.wait_ge(xn_made, TT * (NORM[name] + 1))
                turn_rows(name, 8, lambda kt, t: xn[:, t, kt * P:(kt + 1) * P])
                pe.wait_ge(tp_free, a[name].tp + 8)

            def section(name, hi_s, lo_s):
                s = a[name]
                with pe.Fori(0, s.n) as i:
                    for k in range(8):
                        if k % 4 == 0:
                            gm_free(s.chunk + 2 * i + k // 4)
                        item(s.item + 8 * i + k, s.item + k, hi_s, lo_s, k // 4, k % 4)

            pe.wait_ge(consts, 1)
            pe.wait_ge(rows_in, 16 * 19)
            pe.wait_ge(c_act_made, 1)
            transposes(0, 0, [(prow[0:104, 0, :], 0), (prow[:, 1, :], P), (prow[0:96, 2, :], 2 * P),
                              (crow[:, 1, :], 3 * P)])
            for layer in range(2):
                transposes(1 + layer, (1 + layer) % 2,
                           [(cvrow[:, 4 * layer + k, :], 2 * FT * k) for k in range(4)])
            reduce_mod(0)
            reduce_mod(1)
            turn_norm("norm0")

            s = a["gate"]
            narrow(s.item, s.ms, h_hi, h_lo, RANK)
            pe.wait_ge(ms_free, s.ms + 1)
            transposes(s.tp, s.tp % 2, [(g1[:, t, :], t * P) for t in range(TT)])
            pe.wait_ge(tp_free, s.tp + 1)
            pe.wait_ge(wg_in, 32)
            for f in range(4):
                t, half = f // 2, f % 2
                pe.matmul(ms_open(s.ms + 1 + f), g1_t[0:RANK + 1, t * P:(t + 1) * P],
                          wg2[:, half * W:(half + 1) * W], start=True, stop=True).then_inc(ms_done, 1)
            for f in range(4):
                t, half = f // 2, f % 2
                pe.wait_ge(ms_free, s.ms + 1 + f + 1)
                o = ms_open(s.ms + 5 + f)
                for j in range(4):
                    ins = pe.matmul(o[:, j * P:(j + 1) * P], la[:, t, (4 * half + j) * P:(4 * half + j + 1) * P],
                                    tri[:, :], start=True, stop=True)
                ins.then_inc(ms_done, 1)

            s = a["qk"]

            def turn_qk(i, f):
                pe.wait_ge(u_made, s.chunk + 2 * i + f // 2 + 1)
                transposes(s.tp + 4 * i + f, (s.tp + f) % 2,
                           [(u[:, f // 2, t, (2 * (f % 2) + k) * P:(2 * (f % 2) + k + 1) * P], k * T + t * P)
                            for k in range(2) for t in range(TT)])

            for i in range(2):
                for k in range(8):
                    if k % 4 == 0:
                        gm_free(s.chunk + 2 * i + k // 4)
                    item(s.item + 8 * i + k, s.item + k, h_hi, h_lo, k // 4, k % 4)
                    if i and k < 4:
                        turn_qk(i - 1, k)
            for f in range(4):
                turn_qk(1, f)
            pe.wait_ge(tp_free, s.tp + 8)
            s = a["diag"]
            for hh in range(2):
                o = ms_open(s.ms + hh)
                for hl in range(2):
                    for t in range(TT):
                        c0, tok = (2 * hl + t) * P, slice(t * P, (t + 1) * P)
                        for d in range(2):
                            k = 4 * hh + 2 * hl + d
                            ins = pe.matmul(o[:, c0:c0 + P], qk_t[:, DKT + k, tok], qk_t[:, k, tok],
                                            start=d == 0, stop=d == 1)
                ins.then_inc(ms_done, 1)

            def scores(n):
                w, hh = UNITS[n]
                pe.wait_ge(xq_made, 2 * n + 2)
                o = ms_open(a["v"].ms + n)
                for hl in range(2):
                    for t in range(1 if w == P else TT):
                        c0 = hl * P if w == P else (2 * hl + t) * P
                        for d in range(2):
                            e = ex[:, n % 2, 2 * hl + d, :]
                            key, query = (e[:, 0:P], e[:, P:T]) if w == P else (e[:, t * P:(t + 1) * P],) * 2
                            ins = pe.matmul(o[:, c0:c0 + P], key, query, start=d == 0, stop=d == 1)
                ins.then_inc(ms_done, 1)

            s = a["v"]
            for k in range(16):
                if k % 4 == 0:
                    gm_free(s.chunk + k // 4)
                item(s.item + k, s.item + k, h_hi, h_lo, (k // 4) % 2, k % 4)
                if k:
                    scores(k - 1)
            scores(15)
            reduce_mod(2)
            reduce_mod(3)
            section("r", h_hi, h_lo)
            pe.wait_ge(ms_free, a["v"].ms + 16)
            for h in range(HEADS):
                if h < 2:
                    gm_free(a["gla_out"].chunk + h)
                else:
                    pe.wait_ge(o_gated, h - 1)
                v0, v1 = v_sb[:, 0, h * DV:(h + 1) * DV], v_sb[:, 1, h * DV:(h + 1) * DV]
                pe.matmul(gm[:, h % 2, 0, :], st[:, h, 0, :], v0, start=True, stop=True)
                pe.matmul(gm[:, h % 2, 1, :], sx[:, h, :], v0, start=True, stop=False)
                pe.matmul(gm[:, h % 2, 1, :], st[:, h, 1, :], v1, start=False, stop=True).then_inc(o_ready, 1)
            pe.wait_ge(o_gated, HEADS)
            turn_rows("o", 8, lambda kt, t: r_sb[:, t, kt * P:(kt + 1) * P])
            pe.wait_ge(tp_free, a["o"].tp + 8)
            section("gla_out", h_hi, h_lo)
            reduce_mod(4)

            def turn_pair(layer, g, i, j):
                s = a[f"up{layer}{g}"]
                transposes(s.tp + 4 * i + j, (s.tp + j) % 2,
                           [(u[:, side, t, j * P:(j + 1) * P], side * T + t * P)
                            for side in range(2) for t in range(TT)])

            def ffn(layer, up_groups, down_groups):
                for g, blocks in enumerate(UP_BLOCKS):
                    s = a[f"up{layer}{g}"]

                    def block_(i, turn):
                        for k in range(8):
                            if k % 4 == 0:
                                gm_free(s.chunk + 2 * i + k // 4)
                            item(s.item + 8 * i + k, s.item + k, h_hi, h_lo, k // 4, k % 4)
                            if turn and k < 4:
                                if k == 0:
                                    pe.wait_ge(u_made, s.chunk + 2 * i)
                                turn_pair(layer, g, i - 1, k)

                    block_(0, False)
                    with pe.Fori(1, blocks) as i:
                        block_(i, True)
                    pe.wait_ge(u_made, s.chunk + 2 * blocks)
                    turn_pair(layer, g, blocks - 1, 0)
                    turn_pair(layer, g, blocks - 1, 1)
                    if up_groups[g] is not None:
                        reduce_mod(up_groups[g])
                    tiles = ffn_tiles[f"up{layer}{g}"]
                    s = a[f"down{layer}{g}"]
                    for k in range(16):
                        if k % 4 == 0:
                            gm_free(s.chunk + k // 4)
                        if k < 4:
                            pe.wait_ge(act_lo, tiles + blocks * (k + 1))
                        item(s.item + k, s.item + k, a_hi, a_lo, (k // 4) % 2, k % 4, k_tiles=blocks,
                             total=4 * blocks)
                        if k < 2:
                            turn_pair(layer, g, blocks - 1, k + 2)
                    if down_groups[g] is not None:
                        reduce_mod(down_groups[g])

            turn_norm("norm1")
            ffn(0, (5, 7, None), (6, 8, 9))

            turn_norm("norm2")
            s = a["latent"]
            for k in range(8):
                if k % 4 == 0:
                    gm_free(s.chunk + k // 4)
                src = (a_hi, a_lo) if k < 4 else (h_hi, h_lo)
                item(s.item + k, s.item + k, *src, k // 4, k % 4)
            narrow(s.item + 8, s.ms, a_hi, a_lo, ROPE)
            for name, side in (("norm3", 0), ("norm4", 1)):
                pe.wait_ge(xn_made, TT * (NORM[name] + 1))
                turn_rows(name, 2, lambda kt, t, side=side: u[:, side, t, kt * P:(kt + 1) * P])
            pe.wait_ge(roped, 1)
            fill = a["krope"].tp
            transposes(fill, fill % 2, [(kr[:, t].rearrange("p a b -> p (a b)"), t * P) for t in range(TT)])

            s = a["ukv"]
            pe.wait_ge(tp_free, a["norm4"].tp + 2)

            def turn_keys(k):
                pe.wait_ge(u_made, s.chunk + k + 1)
                transposes(s.tp + k, (s.tp + k) % 2,
                           [(u[:, k % 2, t, hl * P:(hl + 1) * P], hl * T + t * P)
                            for hl in range(2) for t in range(TT)])

            for k in range(8):
                gm_free(s.chunk + k)
                item(s.item + k, s.item + k, ckv_hi, ckv_lo, k % 2, 0, total=LT)
                if k:
                    turn_keys(k - 1)
            turn_keys(7)
            reduce_mod(10)
            q = a["uq"]

            def turn_queries(k):
                pe.wait_ge(u_made, q.chunk + k + 1)
                f = q.tp + 2 * k
                transposes(f, f % 2, [(u[:, k % 2, t, hl * (P + ROPE):hl * (P + ROPE) + P], hl * T + t * P)
                                      for hl in range(2) for t in range(TT)])
                pe.wait_ge(roped, 1 + k + 1)
                transposes(f + 1, (f + 1) % 2, [(qr[:, t].rearrange("p a b -> p (a b)"), t * P)
                                                for t in range(TT)])

            for k in range(8):
                gm_free(q.chunk + k)
                item(q.item + k, q.item + k, cq_hi, cq_lo, k % 2, 0, width=384, total=LT)
                if k:
                    turn_queries(k - 1)
            turn_queries(7)
            reduce_mod(11)

            s = a["heads"]
            pe.wait_ge(tp_free, s.tp)
            for h in range(MH + 2):
                if h < MH:
                    o = ms_open(head_fill(h, False))
                    rope = slice(ROPE * (h % 2), ROPE * (h % 2) + ROPE)
                    for qs, ks, c0 in ((slice(0, P), slice(0, P), 0), (slice(P, T), slice(0, T), P)):
                        v = o[:, c0:c0 + ks.stop]
                        pe.matmul(v, q_t[:, h, qs], k_t[:, h, ks], start=True, stop=False)
                        ins = pe.matmul(v, qr_t[rope, h // 2, qs], kr_t[rope, ks], start=False, stop=True)
                    ins.then_inc(ms_done, 1)
                if 1 <= h <= MH:
                    pe.wait_ge(p_norm, h)
                    f = s.tp + h - 1
                    transposes(f, f % 2, [(probs[:, b, :], b * P) for b in range(3)])
                if h >= 2:
                    o = ms_open(head_fill(h - 2, True))
                    pe.wait_ge(tp_free, s.tp + h - 1)
                    pe.matmul(o[:, 0:T], mv_sb[:, 0, h - 2, :], p_t[:, 0:2, :].rearrange("p b q -> p (b q)"),
                              start=True, stop=False)
                    pe.matmul(o[:, P:T], mv_sb[:, 1, h - 2, :], p_t[:, 2, :],
                              start=False, stop=True).then_inc(ms_done, 1)
            pe.wait_ge(ms_free, s.ms + 2 * MH)
            section("mla_out", o_hi, o_lo)
            reduce_mod(12)
            turn_norm("norm5")
            ffn(1, (13, None, None), (None, None, None))


_INS = ['x', 'c', 'positions', 'mod_w', 'mod_b', 'norm_mix_g', 'norm_ffn_g', 'gla_w_in', 'gla_w_gate2',
        'gla_b_gate', 'gla_head_g', 'gla_w_o', 'kv_norm_g', 'kv_mod_w', 'kv_mod_b', 'mla_w_dkv',
        'mla_kv_norm_g', 'mla_w_ukv', 'mla_w_dq', 'mla_q_norm_g', 'mla_w_uq', 'mla_w_o', 'ffn_w_up',
        'ffn_conv_w', 'ffn_conv_b', 'ffn_w_down', 'final_norm_g']
_OUTS = [((1, 256, 2048), 'float32')]


def kernel(**inputs):
    import numpy as _np
    import concourse.bacc as _bacc
    from concourse import mybir as _mybir
    from concourse.bass_utils import run_bass_kernel_spmd as _run

    nc = _bacc.Bacc("TRN2", target_bir_lowering=False, num_devices=1)
    arrays, args = {}, []
    for name in _INS:
        a = _np.ascontiguousarray(inputs[name])
        arrays[f"in_{name}_dram"] = a
        args.append(nc.dram_tensor(f"in_{name}_dram", a.shape, _mybir.dt.from_np(a.dtype), kind="ExternalInput").ap())
    for i, (shape, dtype) in enumerate(_OUTS):
        dt = _mybir.dt.from_np(_np.dtype(dtype))
        args.append(nc.dram_tensor(f"out_{i}_dram", shape, dt, kind="ExternalOutput").ap())
    yoco_kernel(nc, *args)
    r = _run(nc, [arrays], core_ids=[0])
    got = tuple(r.results[0][f"out_{i}_dram"] for i in range(len(_OUTS)))
    return got[0]
```

```python
from contextlib import ExitStack, contextmanager

import concourse.bass as bass
from concourse import mybir

ALU = mybir.AluOpType
ACT = mybir.ActivationFunctionType
F32 = mybir.dt.float32
F32R = mybir.dt.float32r
I32 = mybir.dt.int32
I8 = mybir.dt.int8
AX_X = mybir.AxisListType.X

P = 128
RAW = 4
AHEAD = 3
MODS = 2
FIRST = 32
KT_ITEM = 4
W = 512
ITEM = KT_ITEM * W
EPS = 1e-6
NEG = -3.0e38
TWO_PI = 6.283185307179586
SPLIT_2PI = (6.28125, round((TWO_PI - 6.28125) * 2 ** 21) / 2 ** 21)
ROUND = 1.5 * 2.0 ** 23

UP_BLOCKS = (4, 4, 3)


def sections():
    s = [
        ("setup", 1, 0, 0, 0, 3, 0),
        ("pre", 1, 0, 32, 0, 0, 2),
        ("norm0", 1, 0, 0, 0, 8, 0),
        ("gate", 1, 1, 0, 0, 0, 9),
        ("qk", 2, 8, 8, 2, 4, 0),
        ("diag", 1, 0, 0, 0, 0, 2),
        ("v", 1, 16, 16, 4, 0, 16),
        ("mod_v", 1, 0, 0, 0, 0, 5),
        ("r", 2, 8, 4, 2, 0, 0),
        ("o", 1, 0, 0, 0, 8, 0),
        ("gla_out", 2, 8, 4, 2, 0, 0),
        ("mod_gla", 1, 0, 0, 0, 0, 1),
        ("norm1", 1, 0, 0, 0, 8, 0),
    ]

    def ffn(layer, up_mods, down_mods, after_up, after_down):
        for g, n in enumerate(UP_BLOCKS):
            s.append((f"up{layer}{g}", n, 8, 0, 2, 4, 0))
            s.append((f"upm{layer}{g}", 1, 0, up_mods[g], 0, 0, 0))
            s.append((f"modu{layer}{g}", 1, 0, 0, 0, 0, after_up[g]))
            s.append((f"down{layer}{g}", 2, 8, down_mods[g], 2, 0, 0))
            s.append((f"modd{layer}{g}", 1, 0, 0, 0, 0, after_down[g]))

    ffn(0, (16, 16, 16), (8, 8, 8), (4, 1, 1), (1, 1, 1))
    s += [
        ("norm2", 1, 0, 0, 0, 8, 0),
        ("latent", 1, 9, 0, 2, 0, 1),
        ("norm3", 1, 0, 0, 0, 2, 0),
        ("norm4", 1, 0, 0, 0, 2, 0),
        ("krope", 1, 0, 0, 0, 1, 0),
        ("ukv", 1, 8, 8, 8, 8, 0),
        ("uq", 1, 8, 8, 8, 16, 0),
        ("mod_uq", 1, 0, 0, 0, 0, 4),
        ("heads", 1, 0, 0, 0, 16, 32),
        ("mla_out", 2, 8, 8, 2, 0, 0),
        ("mod_mla", 1, 0, 0, 0, 0, 1),
        ("norm5", 1, 0, 0, 0, 8, 0),
    ]
    ffn(1, (16, 0, 0), (0, 0, 0), (4, 0, 0), (0, 0, 0))
    return s


class At:

    def __init__(self, counts, n):
        self.item, self.mod, self.chunk, self.tp, self.ms = counts
        self.n = n


def table():
    at, counts = {}, [0] * 5
    for name, n, *per in sections():
        at[name] = At(counts, n)
        counts = [c + n * p for c, p in zip(counts, per)]
    at["end"] = At(counts, 0)
    return at


class Steps:

    def __init__(self, eng, sem):
        self.eng, self.sem, self.base, self.n = eng, sem, 0, 0

    def mark(self, ins):
        ins.then_inc(self.sem, 1)
        self.n += 1
        return self.base + self.n

    def wait(self, value):
        self.eng.wait_ge(self.sem, value)

    def link(self, ins):
        self.wait(self.mark(ins))

    @contextmanager
    def loop(self, i, start, end, per):
        first = self.base + self.n
        self.base, self.n = first + (i - start) * per, 0
        yield
        assert self.n == per, (self.n, per)
        self.base, self.n = first + (end - start) * per, 0


def yoco_kernel(nc, x, c, positions, mod_w, mod_b, norm_mix_g, norm_ffn_g, gla_w_in, gla_w_gate2,
                gla_b_gate, gla_head_g, gla_w_o, kv_norm_g, kv_mod_w, kv_mod_b, mla_w_dkv,
                mla_kv_norm_g, mla_w_ukv, mla_w_dq, mla_q_norm_g, mla_w_uq, mla_w_o, ffn_w_up,
                ffn_conv_w, ffn_conv_b, ffn_w_down, final_norm_g, out):
    _, T, D = x.shape
    TT = T // P
    KT = D // P
    HEADS = gla_head_g.shape[1]
    DV = gla_head_g.shape[2]
    RANK = gla_w_gate2.shape[1]
    HK = gla_w_gate2.shape[2]
    DKT = HK // P
    DK = HK // HEADS
    GATE_NORM = 16.0
    LAT = mla_w_ukv.shape[0]
    LT = LAT // P
    MH = D // P
    ROPE = mla_w_dkv.shape[1] - LAT
    HR = ROPE // 2
    FF = ffn_w_down.shape[1]
    FT = FF // P
    MSCALE = float(P + ROPE) ** -0.5
    assert TT == 2 and KT == 16 and DKT == 8 and LT == 4 and DV == W and sum(UP_BLOCKS) * W == FF
    assert DK ** -0.5 == 0.25 * 0.25
    at = table()
    TOTAL = at["end"].item

    base = (nc.sbuf_base + 63) // 64 * 64

    def place(name, offset, shape, dt):
        return nc.alloc_sbuf_tensor_at(name, shape, dt, offset=base + offset)

    K16 = 16384
    X, S1, S2, RW, MD, WS, AC, GU, PR = 0, K16, 3 * K16, 5 * K16, 7 * K16, 8 * K16, 10 * K16, 11 * K16, 12 * K16
    x_sb = place("x_sb", X, [P, TT, D], F32)
    h_hi = place("h_hi", S1, [P, KT, T], F32R)
    h_lo = place("h_lo", S1 + K16, [P, KT, T], F32R)
    a_hi = place("a_hi", S2, [P, KT, T], F32R)
    a_lo = place("a_lo", S2 + K16, [P, KT, T], F32R)
    raw = place("raw", RW, [P, RAW, ITEM], F32)
    w_lo = place("w_lo", RW, [P, RAW, ITEM], F32R)
    mods = place("mods", MD, [P, MODS, D], F32)
    w_hi = place("w_hi", WS, [P, RAW, ITEM], F32R)
    acc = place("acc", AC, [P, 2, D], F32)
    gate_b = place("gate_b", GU, [P, D], F32)
    u = place("u", GU + 8192, [P, 2, TT, W], F32)
    xn = place("xn", GU, [P, TT, D], F32)
    prow = place("prow", S2, [P, 3, P], F32)
    crow = place("crow", S2 + 2048, [KT, 2, P], F32)
    cvrow = place("cvrow", S2 + 4096, [2 * FT, 8, P], F32)
    qk_t = place("qk_t", X, [P, 2 * DKT, T], F32)
    v_sb = place("v_sb", S2, [P, TT, D], F32)
    r_sb = place("r_sb", S2 + K16, [P, TT, D], F32)
    b_sb = place("b_sb", GU, [P, DKT, T], F32)
    la = place("la", GU + 8192, [P, TT, HK], F32)
    ex = place("ex", GU + 8192, [P, 2, DKT // 2, T], F32)
    q_t = place("q_t", S1, [P, MH, T], F32)
    k_t = place("k_t", S1 + K16, [P, MH, T], F32)
    o_hi = place("o_hi", S1, [P, MH, T], F32R)
    o_lo = place("o_lo", S1 + K16, [P, MH, T], F32R)
    mv_sb = place("mv_sb", S2, [P, TT, MH, P], F32)
    qr_t = place("qr_t", S2 + K16, [P, MH // 2, T], F32)
    cq_hi = place("cq_hi", S2 + K16 + 8192, [P, LT, T], F32R)
    cq_lo = place("cq_lo", S2 + K16 + 12288, [P, LT, T], F32R)
    ckv_hi = place("ckv_hi", GU, [P, LT, T], F32R)
    ckv_lo = place("ckv_lo", GU + 4096, [P, LT, T], F32R)
    y_out = place("y_out", S1, [P, TT, D], F32)

    cursor = [PR]

    def keep(name, shape, dt):
        n = 1
        for d in shape[1:]:
            n *= d
        n = (n * (1 if dt == I8 else 4) + 31) // 32 * 32
        t = place(name, cursor[0], shape, dt)
        cursor[0] += n
        return t

    ident = keep("ident", [P, P], F32)
    ones = keep("ones", [P, P], F32)
    tri = keep("tri", [P, P], F32)
    pcol = keep("pcol", [P, 3, P], F32)
    c_col = keep("c_col", [P, KT], F32)
    cv_col = keep("cv_col", [P, 2, 4, 2 * FT], F32)
    modc = keep("modc", [P, 2, KT], F32)
    ab = keep("ab", [P, 10, KT], F32)
    stats = keep("stats", [P, 3, 16], F32)
    half_neg = keep("half_neg", [P, 16], F32)
    pos_i = keep("pos_i", [P, TT], I32)
    pos_f = keep("pos_f", [P, TT], F32)
    inv = keep("inv", [P, HR], F32)
    cos = keep("cos", [P, TT, HR], F32)
    sin = keep("sin", [P, TT, HR], F32)
    TMP = cursor[0]
    limit = nc.sbuf_usable_end - base

    def tmp(name, offset, shape, dt):
        return place(name, TMP + offset, shape, dt)

    conv = tmp("conv", 0, [P, 2, 2, T], F32)
    gated = tmp("gated", 4096, [P, 2, T], F32)
    both = tmp("both", 5120, [P, 2, T], F32)
    ang = tmp("ang", 7168, [P, 3, TT, HR], F32)
    st = tmp("st", 0, [P, HEADS, TT, P], F32)
    sx = tmp("sx", 4096, [P, HEADS, P], F32)
    mask = tmp("mask", 6144, [P, 8, P], I8)
    wg2 = tmp("wg2", 0, [RANK + 1, HK], F32)
    g1_t = tmp("g1_t", 4096, [32, T], F32)
    sc = place("sc", GU + 8192, [P, 3, P], F32)
    probs = tmp("probs", 0, [P, 2, 3, P], F32)
    p_t = tmp("p_t", 3072, [P, 3, P], F32)
    kr_t = tmp("kr_t", 4608, [P, T], F32)
    causal = tmp("causal", 5632, [P, 3, P], F32)
    rt = tmp("rt", 0, [P, 4, TT, 2, HR], F32)
    qr = tmp("qr", 2048, [P, TT, 2, ROPE], F32)
    kr = tmp("kr", 3072, [P, TT, 2, ROPE], F32)
    junk = place("junk", GU, [P, TT, W], F32)
    assert TMP + 7936 <= limit, (TMP + 7936, limit)

    MIX, FFN, KVN, HEAD, KVL, QL = 0, 32, 64, 80, 96, 100
    A_OF = {"mix0": 0, "ffn0": 2, "kv": 4, "mix1": 6, "ffn1": 8}

    PART1 = {8: 0, 9: 1, 10: 3, 11: 2, 12: 4, 13: 5}

    def mod_source(g):
        if g in (6, 7):
            return kv_mod_w, (g - 6) * D
        layer, j = (0, g) if g < 6 else (1, PART1[g])
        return mod_w[layer], j * D

    def mod_bias(g):
        if g in (6, 7):
            return 1, 96 + (g - 6) * KT
        return (1, g * KT) if g < 6 else (2, PART1[g] * KT)

    GATES = (2, 5, 11, 13)
    REDUCE = {0: ("pre", 0), 1: ("pre", 1), 2: ("mod_v", 0), 3: ("mod_v", 4), 4: ("mod_gla", 0),
              5: ("modu00", 0), 6: ("modd00", 0), 7: ("modu01", 0), 8: ("modd01", 0), 9: ("modu02", 0),
              10: ("modd02", 0), 11: ("mod_uq", 0), 12: ("mod_mla", 0), 13: ("modu10", 0)}
    SHIFT = {0: ("mix0", MIX), 3: ("ffn0", FFN), 6: ("kv", KVN), 8: ("mix1", MIX + KT), 10: ("ffn1", FFN + KT)}
    SCALE = {1: ("mix0", MIX), 4: ("ffn0", FFN), 7: ("kv", KVN), 9: ("mix1", MIX + KT), 12: ("ffn1", FFN + KT)}

    def fills_of(g):
        return 4 if g in GATES else 1

    def reduce_at(g):
        name, k = REDUCE[g]
        return at[name].ms + k

    with ExitStack() as ctx:
        def sem(name):
            return ctx.enter_context(nc.semaphore(name))

        gm = ctx.enter_context(nc.psum_tensor("gm", [P, 2, TT, W], F32))
        tp = ctx.enter_context(nc.psum_tensor("tp", [P, 2, W], F32))
        ms = ctx.enter_context(nc.psum_tensor("ms", [P, 2, W], F32))

        raw_in = [sem(f"raw_in{i}") for i in range(RAW)]
        mod_in = [sem(f"mod_in{i}") for i in range(MODS)]
        first_in = [sem(f"first_in{i}") for i in range(MODS + RAW)]
        rows_in = sem("rows_in")
        x_in = sem("x_in")
        gate_in = sem("gate_in")
        wg_in = sem("wg_in")
        out_in = sem("out_in")
        consts = sem("consts")
        hi_made = sem("hi_made")
        lo_made = sem("lo_made")
        item_used = sem("item_used")
        mod_used = sem("mod_used")
        acc_zero = sem("acc_zero")
        u_made = sem("u_made")
        tp_done = sem("tp_done")
        tp_free = sem("tp_free")
        ms_done = sem("ms_done")
        ms_free = sem("ms_free")
        x_added = sem("x_added")
        sums = sem("sums")
        rstd = sem("rstd")
        xn_made = sem("xn_made")
        split_hi = sem("split_hi")
        act_step = sem("act_step")
        dve_step = sem("dve_step")
        pool_step = sem("pool_step")
        c_act_made = sem("c_act_made")
        params = sem("params")
        columns_on = sem("columns_on")
        taps = sem("taps")
        conv_made = sem("conv_made")
        silu_made = sem("silu_made")
        gated_made = sem("gated_made")
        act_hi = sem("act_hi")
        act_lo = sem("act_lo")
        z_log = sem("z_log")
        e_made = sem("e_made")
        f_made = sem("f_made")
        xq_made = sem("xq_made")
        o_ready = sem("o_ready")
        o_sums = sem("o_sums")
        o_rstd = sem("o_rstd")
        o_gated = sem("o_gated")
        ang_made = sem("ang_made")
        sin_made = sem("sin_made")
        roped = sem("roped")
        s_made = sem("s_made")
        p_made = sem("p_made")
        p_norm = sem("p_norm")
        p_evac = sem("p_evac")
        o_split = sem("o_split")
        o_done = sem("o_done")

        block = ctx.enter_context(nc.Block())

        def halves(v, w, half):
            return v.rearrange("p t (g h r) -> p (t g) h r", h=2, r=w)[:, :, half, :]

        def head_fill(h, output):
            if output:
                k = 2 * h + 3 if h + 2 < MH else MH + h
            else:
                k = h if h < 2 else 2 * h - 2
            return at["heads"].ms + k

        LEVELS = [64, 32, 16, 8, 4, 2, 1]
        UNITS = [(P, 0), (P, 1)] + [(w, hh) for w in LEVELS for hh in (0, 1)]
        ffn_tiles = {}
        n = 0
        for layer in range(2):
            for g, blocks in enumerate(UP_BLOCKS):
                ffn_tiles[f"up{layer}{g}"] = n
                n += 4 * blocks
        added = {"gla_out": 0, "down00": 4, "down01": 8, "down02": 12, "mla_out": 16,
                 "down10": 20, "down11": 24, "down12": 28, "end": 32}
        def first_slot(n):
            k = n % (MODS + RAW)
            return mods[:, k, :] if k < MODS else raw[:, k - MODS, :]

        def up_bare(mods_per, blocks):
            return blocks - KT // mods_per if mods_per else 0

        def mod_positions():
            spread = (("qk", 2, 8, 0, 0), ("v", 3, 8, 0, 0), ("r", 4, 4, 0, 0), ("gla_out", 4, 4, 8, 0),
                      ("up00", 5, 4, 0, 0), ("down00", 6, 8, 0, 0), ("up01", 7, 4, 0, 0), ("down01", 8, 8, 0, 0),
                      ("up02", 9, 8, 0, up_bare(8, UP_BLOCKS[2])), ("down02", 10, 8, 0, 0),
                      ("ukv", 11, 8, 0, 0), ("uq", 11, 8, 8, 0), ("mla_out", 12, 8, 0, 0), ("up10", 13, 4, 0, 0))
            found, n = {}, FIRST
            for name, g, per, kt, bare in spread:
                for k in range(8 * bare, {"ukv": 8, "uq": 8, "v": 16}.get(name, 16 if "down" in name else 8 * at[name].n)):
                    if k % 8 >= 8 - per:
                        found[at[name].item + k] = (n, g, kt)
                        n, kt = n + 1, kt + 1
            assert n == at["end"].mod
            return found

        NORM = {"norm0": 0, "norm1": 1, "norm2": 2, "norm3": 3, "norm4": 4, "norm5": 5, "final": 6}

        splits = {"norm0": 0, "o": 8, "norm1": 16, "norm2": 24, "norm3": 32, "norm4": 34, "norm5": 36}

        NARROW = {at["gate"].item: KT * RANK, at["latent"].item + 8: KT * ROPE}
        for k in range(8):
            NARROW[at["uq"].item + k] = KT_ITEM * 384
        for k in range(16):
            NARROW[at["down02"].item + k] = NARROW[at["down12"].item + k] = UP_BLOCKS[2] * W

        def words_of(n):
            return NARROW.get(n, ITEM) if isinstance(n, int) else ITEM

        def made(fill):
            return fill + 1 - (fill > at["gate"].ms) - (fill > at["latent"].ms)

        @block.sync
        def _(sp):
            a = at

            def load_item(n, src):
                if n < RAW:
                    sp.wait_ge(mod_used, max(m for m in range(FIRST) if m % (MODS + RAW) == MODS + n) + 1)
                else:
                    sp.wait_ge(item_used, n - RAW + 1)
                _, j, width = src.shape
                dst = raw[:, n % RAW, 0:j * width].rearrange("p (j n) -> p j n", j=j)
                sp.dma_start(dst, src).then_inc(raw_in[n % RAW], 16)

            def load_mod(n, g, kt):
                sp.wait_ge(mod_used, n - MODS + 1)
                w, col = mod_source(g)
                sp.dma_start(mods[:, n % MODS, :], w[kt * P:kt * P + P, col:col + D])\
                    .then_inc(mod_in[n % MODS], 16)

            def load_first(n):
                ring = MODS + RAW
                if n >= ring:
                    sp.wait_ge(mod_used, n - ring + 1)
                w, col = mod_source(n // KT)
                sp.dma_start(first_slot(n), w[n % KT * P:(n % KT + 1) * P, col:col + D])\
                    .then_inc(first_in[n % ring], 16)

            def columns(w, q, col, k_tiles=KT_ITEM, width=W):
                rows = w[q * k_tiles * P:(q + 1) * k_tiles * P, col:col + width]
                return rows.rearrange("(j p) n -> p j n", p=P)

            def up_down(layer):
                up, down, f0, out_ = ffn_w_up[layer], ffn_w_down[layer], 0, []
                for blocks in UP_BLOCKS:
                    out_ += [columns(up, q, f0 + W * i + FF * side)
                             for i in range(blocks) for side in range(2) for q in range(4)]
                    part = down[f0:f0 + blocks * W, :]
                    out_ += [columns(part, q, W * ch, blocks) for ch in range(4) for q in range(4)]
                    f0 += blocks * W
                return out_

            def square(w, col=0):
                return [columns(w, q, col + W * ch) for ch in range(4) for q in range(4)]

            for src, tile_, row in (
                (norm_mix_g, 0, MIX), (norm_ffn_g, 0, FFN), (kv_norm_g, 0, KVN),
                (gla_head_g, 0, HEAD), (mla_kv_norm_g, 0, KVL), (mla_q_norm_g, 0, QL),
                (mod_b[0], 1, 0), (kv_mod_b, 1, 96), (mod_b[1], 2, 0),
            ):
                names = "abcd"[:len(src.shape)]
                flat = src if len(names) == 1 else src.rearrange(" ".join(names) + " -> (" + " ".join(names) + ")")
                v = flat.rearrange("(r p) -> r p", p=P)
                sp.dma_start(prow[row:row + v.shape[0], tile_, :], v).then_inc(rows_in, 16)
            sp.dma_start(crow[:, 0, :], c.rearrange("o (r p) -> (o r) p", p=P)).then_inc(rows_in, 16)
            sp.dma_start(pos_i[:, :], positions.rearrange("o (t p) -> p (o t)", p=P),
                         allow_slow_non_contiguous=True).then_inc(rows_in, 16)
            for n in range(2):
                load_first(n)
            sp.dma_start(x_sb[:, :, :], x.rearrange("o (t p) d -> p (o t) d", p=P)).then_inc(x_in, 16)
            for layer in range(2):
                for k in range(3):
                    sp.dma_start(cvrow[:, 4 * layer + k, :],
                                 ffn_conv_w[layer, k].rearrange("(r p) -> r p", p=P)).then_inc(rows_in, 16)
                sp.dma_start(cvrow[:, 4 * layer + 3, :],
                             ffn_conv_b[layer].rearrange("(r p) -> r p", p=P)).then_inc(rows_in, 16)
            for n in range(2, FIRST):
                load_first(n)

            w_in = gla_w_in[0]
            where = [w_in[:, 2 * HK + 2 * D:].rearrange("(j p) n -> p j n", p=P)]
            where += square(w_in) + square(w_in, 2 * HK) + square(w_in, 2 * HK + D) + square(gla_w_o[0])
            where += up_down(0)
            where += [columns(mla_w_dkv, q, 0) for q in range(4)] + [columns(mla_w_dq[0], q, 0) for q in range(4)]
            where += [mla_w_dkv[:, LAT:].rearrange("(j p) n -> p j n", p=P)]
            where += [columns(mla_w_ukv, 0, W * k) for k in range(8)]
            where += [columns(mla_w_uq[0], 0, 384 * k, KT_ITEM, 384) for k in range(8)]
            where += square(mla_w_o[0])
            where += up_down(1)
            assert len(where) == TOTAL
            mod_at = mod_positions()
            for n, src in enumerate(where):
                if n - AHEAD in mod_at:
                    load_mod(*mod_at[n - AHEAD])
                if n == a["r"].item + 8:
                    sp.wait_ge(ms_done, made(a["diag"].ms + 1))
                    sp.wait_ge(xq_made, 2 * len(UNITS))
                    sp.dma_start(x_sb[:, :, :], x.rearrange("o (t p) d -> p (o t) d", p=P)).then_inc(x_in, 16)
                load_item(n, src)
                if n == 0:
                    sp.dma_start(wg2[0:RANK, :], gla_w_gate2[0]).then_inc(wg_in, 16)
                    sp.dma_start(wg2[RANK:RANK + 1, :], gla_b_gate).then_inc(wg_in, 16)

            sp.wait_ge(x_added, added["end"])
            sp.dma_start(gate_b[:, :], final_norm_g.partition_broadcast(P)).then_inc(gate_in, 16)
            o_v = out.rearrange("o (t p) d -> p (o t) d", p=P)
            for t in range(TT):
                sp.wait_ge(xn_made, 2 * NORM["final"] + t + 1)
                sp.dma_start(o_v[:, t, :], y_out[:, t, :]).then_inc(out_in, 16)
            sp.wait_ge(out_in, 16 * TT)

        @block.gpsimd
        def _(pool):
            step = Steps(pool, pool_step)
            step.mark(pool.memset(ident[:, :], 0.0))
            step.mark(pool.memset(ones[:, :], 1.0))
            step.mark(pool.memset(tri[:, :], 1.0))
            step.mark(pool.memset(half_neg[:, :], -0.5))
            step.mark(pool.memset(g1_t[:, :], 1.0))
            for k in range(HR):
                step.mark(pool.memset(inv[:, k:k + 1], float(10000.0 ** (-2.0 * k / ROPE))))
            step.wait(step.base + step.n)
            step.mark(pool.affine_select(out=ident[:, :], in_=ident[:, :], pattern=[[-1, P]],
                                         compare_op=ALU.not_equal, fill=1.0, base=0, channel_multiplier=1))
            pool.affine_select(out=tri[:, :], in_=tri[:, :], pattern=[[1, P]], compare_op=ALU.is_ge,
                               fill=0.0, base=0, channel_multiplier=-1).then_inc(consts, 1)
            for g in range(2):
                pool.memset(acc[:, g, :], 0.0).then_inc(acc_zero, 1)

            def clear(g):
                pool.wait_ge(ms_done, made(reduce_at(g - 2) + fills_of(g - 2) - 1))
                pool.memset(acc[:, g % 2, :], 0.0).then_inc(acc_zero, 1)

            def root(index, count, width, ready, ready_at, signal):
                pool.wait_ge(ready, ready_at)
                src, dst = stats[:, 0, index:index + count], stats[:, 1, index:index + count]
                step.link(pool.tensor_scalar(dst, src, 1.0 / width, EPS, ALU.mult, ALU.add))
                pool.tensor_tensor(dst, dst, half_neg[:, 0:count], ALU.pow).then_inc(signal, 1)

            def norm_root(name, width):
                root(TT * (NORM[name] % 2), TT, width, sums, TT * (NORM[name] + 1), rstd)

            norm_root("norm0", D)
            clear(2)
            pool.wait_ge(tp_free, at["norm0"].tp + 8)
            for k, w in enumerate(LEVELS):
                view = mask[:, k, :].rearrange("p (g h r) -> p g h r", h=2, r=w)[:, :, 1, :]
                step.link(pool.memset(mask[:, k, :], 0))
                step.link(pool.memset(view, 1))
                blocks = P // (2 * w)
                step.link(pool.affine_select(out=view, in_=view, pattern=[[-2 * w, blocks], [0, w]],
                                             compare_op=ALU.is_ge, fill=0.0, base=0, channel_multiplier=1))
                step.link(pool.affine_select(out=view, in_=view, pattern=[[2 * w, blocks], [0, w]],
                                             compare_op=ALU.is_ge, fill=0.0, base=w - 1, channel_multiplier=-1))
            step.link(pool.memset(mask[:, 7, :], 0))
            pool.affine_select(out=mask[:, 7, :], in_=mask[:, 7, :], pattern=[[-1, P]],
                               compare_op=ALU.not_equal, fill=1.0, base=0,
                               channel_multiplier=1).then_inc(consts, 1)
            clear(3)
            for n, (w, hh) in enumerate(UNITS):
                pool.wait_ge(f_made, n + 1)
                for half in range(2):
                    f, s = halves(ex[:, n % 2], w, half), halves(
                        qk_t[:, (0 if half else DKT) + 4 * hh:(0 if half else DKT) + 4 * hh + 4, :], w, half)
                    pool.tensor_tensor(f, f, s, ALU.mult).then_inc(xq_made, 1)
            clear(4)
            for h in range(HEADS):
                root(TT * h, TT, DV, o_sums, TT * (h + 1), o_rstd)
            norm_root("norm1", D)
            for g in range(5, 12):
                clear(g)
            norm_root("norm2", D)
            norm_root("norm3", LAT)
            norm_root("norm4", LAT)
            clear(12)
            pool.wait_ge(tp_free, at["norm4"].tp + 2)
            step.link(pool.memset(causal[:, :, :], 0.0))
            for k in (0, 2):
                ins = pool.affine_select(out=causal[:, k, :], in_=causal[:, k, :], pattern=[[-1, P]],
                                         compare_op=ALU.is_ge, fill=NEG, base=0, channel_multiplier=1)
                step.mark(ins) if k == 0 else ins.then_inc(consts, 1)
            clear(13)
            norm_root("norm5", D)
            norm_root("final", D)

        @block.scalar
        def _(act):
            a = at
            step = Steps(act, act_step)

            def hi(n, slot=None):
                if isinstance(n, int) and n >= TOTAL:
                    return
                k, words = n if slot is None else slot, words_of(n)
                act.wait_ge(raw_in[k % RAW], 16 * ((n - k % RAW) // RAW + 1) if isinstance(n, int)
                            else 4 * (n - k % RAW) + 16)
                act.activation(w_hi[:, k % RAW, 0:words], raw[:, k % RAW, 0:words],
                               ACT.Copy).then_inc(hi_made, 1)

            def evac(last_item, par, dst, src=None, func=ACT.Copy):
                act.wait_ge(item_used, last_item + 1)
                act.activation(dst, gm[:, par] if src is None else src, func).then_inc(u_made, 1)

            def split(fill, count, dst, scale, shift):
                for f in range(count):
                    act.wait_ge(tp_done, fill + f + 1)
                    for k in range(2):
                        for d, sc_, sh_ in zip(dst, scale, shift):
                            kt = 2 * f + k
                            ins = act.activation(
                                d[:, kt, :], tp[:, (fill + f) % 2, k * T:(k + 1) * T], ACT.Identity,
                                scale=sc_[:, kt:kt + 1], bias=0.0 if sh_ is None else sh_[:, kt:kt + 1])
                    ins.then_inc(split_hi, 1)

            def squares(name, src, spare):
                for t in range(TT):
                    k = TT * (NORM[name] % 2) + t
                    act.activation(spare[:, t, :], src[:, t, :], ACT.Square,
                                   accum_out=stats[:, 0, k:k + 1]).then_inc(sums, 1)

            def load_gate(layer, part):
                act.dma_start(gate_b[:, :], mod_b[layer, part * D:(part + 1) * D].partition_broadcast(P))\
                   .then_inc(gate_in, 16)

            def normalised(name):
                act.wait_ge(rstd, NORM[name] + 1)
                k = TT * (NORM[name] % 2) + 1
                act.activation(xn[:, 1, :], x_sb[:, 1, :], ACT.Identity, scale=stats[:, 1, k:k + 1],
                               bias=0.0).then_inc(xn_made, 1)

            act.wait_ge(rows_in, 16 * 19)
            act.activation(crow[:, 1, :], crow[:, 0, :], ACT.Silu).then_inc(c_act_made, 1)
            act.wait_ge(ang_made, 1)
            act.activation(sin[:, :, :], ang[:, 0], ACT.Sin).then_inc(sin_made, 1)
            act.activation(cos[:, :, :], ang[:, 1], ACT.Sin).then_inc(sin_made, 1)
            act.wait_ge(x_in, 16)
            squares("norm0", x_sb, xn)
            normalised("norm0")
            act.wait_ge(columns_on, 1)
            split(a["norm0"].tp, 8, (h_hi,), (ab[:, A_OF["mix0"]],), (ab[:, A_OF["mix0"] + 1],))
            for n in range(AHEAD + 1):
                hi(n)
            def gate_logs(f):
                s = a["gate"]
                t, half = f // 2, f % 2
                v = la[:, t, half * W:(half + 1) * W]
                act.wait_ge(ms_done, made(s.ms + 1 + f))
                step.link(act.activation(v, ms[:, (s.ms + 1 + f) % 2, :], ACT.Abs))
                step.link(act.activation(v, v, ACT.Exp, scale=-1.0))
                act.activation(v, v, ACT.Ln, bias=1.0).then_inc(z_log, 1)

            s = a["qk"]
            for i in range(2):
                for k in range(8):
                    hi(s.item + AHEAD + 8 * i + k)
                    if i == 0 and k in (1, 2):
                        gate_logs(2 * k - 2)
                        gate_logs(2 * k - 1)
                    if k % 4 == 3:
                        par = k // 4
                        if par == 0:
                            act.wait_ge(ms_done, made(a["gate"].ms + 8))
                        act.wait_ge(tp_done, s.tp + 4 * i)
                        evac(s.item + 8 * i + k, par, u[:, par])
            s = a["v"]
            for k in range(16):
                hi(s.item + AHEAD + k)
                w, hh = UNITS[k]
                act.wait_ge(e_made, k + 1)
                act.activation(ex[:, k % 2], ex[:, k % 2], ACT.Exp, scale=1.0 / GATE_NORM).then_inc(f_made, 1)
                if k % 4 == 3:
                    ch = k // 4
                    evac(s.item + k, ch % 2, v_sb[:, :, ch * W:(ch + 1) * W])
            load_gate(0, 2)
            s = a["r"]
            with act.Fori(0, s.n) as i:
                for k in range(8):
                    hi(s.item + AHEAD + 8 * i + k, s.item + AHEAD + k)
                    if k % 4 == 3:
                        par = k // 4
                        evac(s.item + 8 * i + k, par, r_sb[:, :, bass.ds(1024 * i + par * W, W)],
                             func=ACT.Silu)
            for h in range(HEADS):
                act.wait_ge(o_ready, h + 1)
                for t in range(TT):
                    act.activation(ex[:, h % 2, 2 * t:2 * t + 2, :], gm[:, h % 2, t].rearrange("p (a b) -> p a b", a=2),
                                   ACT.Square, accum_out=stats[:, 0, TT * h + t:TT * h + t + 1])\
                       .then_inc(o_sums, 1)
            split(a["o"].tp, 8, (h_hi,), (pcol[:, 0, HEAD:HEAD + KT],), (None,))

            def add_section(name):
                s = a[name]

                def body(i):
                    for k in range(8):
                        if k % 4 == 3:
                            par = k // 4
                            if not (isinstance(i, int) and added[name] + 2 * i == 0):
                                act.wait_ge(x_added, added[name] + 2 * i)
                            evac(s.item + 8 * i + k, par, u[:, par])
                        hi(s.item + AHEAD + 8 * i + k, s.item + AHEAD + k)

                if added[name] == 0:
                    for i in range(s.n):
                        body(i)
                else:
                    with act.Fori(0, s.n) as i:
                        body(i)

            add_section("gla_out")
            act.wait_ge(x_added, added["down00"])
            squares("norm1", x_sb, xn)
            normalised("norm1")
            act.wait_ge(columns_on, 2)
            split(a["norm1"].tp, 8, (h_hi,), (ab[:, A_OF["ffn0"]],), (ab[:, A_OF["ffn0"] + 1],))

            def conv_tile(layer, g, blk, j, fill, tile_):
                s = a[f"up{layer}{g}"]
                bank = (s.tp + j) % 2
                ft = sum(UP_BLOCKS[:g]) * 4 + j
                act.wait_ge(tp_done, fill + 1)
                for side in range(2):
                    col = 4 * blk + (ft + side * FT)
                    cs = slice(col, col + 1) if isinstance(col, int) else bass.ds(col, 1)
                    ins = act.activation(conv[:, j % 2, side, :], tp[:, bank, side * T:(side + 1) * T],
                                         ACT.Identity, scale=cv_col[:, layer, 2, cs], bias=cv_col[:, layer, 3, cs])
                ins.then_inc(taps, 1)

            def conv_silu(j, tile_):
                act.wait_ge(conv_made, tile_ + 1)
                act.activation(conv[:, j % 2, 1, :], conv[:, j % 2, 1, :], ACT.Silu).then_inc(silu_made, 1)

            def conv_hi(blk, j, tile_):
                act.wait_ge(gated_made, tile_ + 1)
                kt = 4 * blk + j
                d = a_hi[:, kt, :] if isinstance(kt, int) else a_hi[:, bass.ds(kt, 1), :]
                s_ = gated[:, j % 2, :] if isinstance(kt, int) else gated[:, j % 2:j % 2 + 1, :]
                act.activation(d, s_, ACT.Copy).then_inc(act_hi, 1)

            def up(layer, g):
                s = a[f"up{layer}{g}"]
                t0 = ffn_tiles[f"up{layer}{g}"]

                def body(i, conv_too):
                    for k in range(8):
                        if not conv_too and k == 3 and g > 0:
                            act.wait_ge(x_added, added[f"down{layer}{g - 1}"] + 4)
                        if k == 7:
                            evac(s.item + 8 * i + k, 1, u[:, 1])
                        tile_ = t0 + 4 * (i - 1) + k
                        if conv_too and k < 4:
                            conv_tile(layer, g, i - 1, k, s.tp + 4 * (i - 1) + k, tile_)
                        hi(s.item + AHEAD + 8 * i + k, s.item + AHEAD + k)
                        if conv_too and 1 <= k <= 4:
                            conv_hi(i - 1, k - 1, tile_ - 1)
                        if conv_too and k < 4:
                            conv_silu(k, tile_)
                        if k == 3:
                            if conv_too:
                                act.wait_ge(tp_done, s.tp + 4 * i)
                            evac(s.item + 8 * i + k, 0, u[:, 0])

                body(0, False)
                if g == 0:
                    load_gate(layer, 5)
                if g == 2:
                    for i in range(1, s.n):
                        body(i, True)
                else:
                    with act.Fori(1, s.n) as i:
                        body(i, True)

            def last_taps(layer, g, k):
                s, n = a[f"up{layer}{g}"], UP_BLOCKS[g] - 1
                tile_ = ffn_tiles[f"up{layer}{g}"] + 4 * n + k
                conv_tile(layer, g, n, k, s.tp + 4 * n + k, tile_)

            def last_silu(layer, g, k):
                conv_silu(k, ffn_tiles[f"up{layer}{g}"] + 4 * (UP_BLOCKS[g] - 1) + k)

            def last_hi(layer, g, k):
                n = UP_BLOCKS[g] - 1
                conv_hi(n, k, ffn_tiles[f"up{layer}{g}"] + 4 * n + k)

            def down(layer, g):
                name = f"down{layer}{g}"
                s = a[name]
                for k in range(16):
                    if k % 4 == 3:
                        ch = k // 4
                        if ch >= 2:
                            act.wait_ge(x_added, added[name] + ch - 1)
                        evac(s.item + k, ch % 2, u[:, ch % 2])
                    hi(s.item + AHEAD + k)
                    if k < 2:
                        for step_of in (last_taps, last_silu, last_hi):
                            for j in (2 * k, 2 * k + 1):
                                step_of(layer, g, j)

            for g in range(3):
                up(0, g)
                down(0, g)
            act.wait_ge(x_added, added["mla_out"])
            squares("norm2", x_sb, xn)
            normalised("norm2")
            act.wait_ge(columns_on, 4)
            split(a["norm2"].tp, 8, (h_hi, a_hi), (ab[:, A_OF["mix1"]], ab[:, A_OF["kv"]]),
                  (ab[:, A_OF["mix1"] + 1], ab[:, A_OF["kv"] + 1]))
            s = a["latent"]
            for k in range(9):
                hi(s.item + AHEAD + k)
                if k in (3, 7):
                    evac(s.item + k, k // 4, u[:, k // 4])
                    act.wait_ge(u_made, s.chunk + k // 4 + 1)
                    squares("norm3" if k == 3 else "norm4", u[:, k // 4], junk)
            split(a["norm3"].tp, 2, (ckv_hi,), (pcol[:, 0, KVL:KVL + LT],), (None,))
            split(a["norm4"].tp, 2, (cq_hi,), (pcol[:, 0, QL:QL + LT],), (None,))
            s = a["ukv"]
            for k in range(8):
                hi(s.item + AHEAD + k)
                act.wait_ge(item_used, s.item + k + 1)
                if k >= 2:
                    act.wait_ge(tp_done, s.tp + k - 1)
                else:
                    act.wait_ge(tp_done, a["norm4"].tp + 2)
                src = gm[:, k % 2].rearrange("p t (h v n) -> p t h v n", h=2, v=2)
                act.activation(u[:, k % 2, :, 0:2 * P].rearrange("p t (h n) -> p t h n", h=2),
                               src[:, :, :, 0, :], ACT.Copy)
                act.activation(mv_sb[:, :, 2 * k:2 * k + 2, :], src[:, :, :, 1, :], ACT.Copy).then_inc(u_made, 1)
            load_gate(1, 2)
            s = a["uq"]
            for k in range(8):
                hi(s.item + AHEAD + k)
                act.wait_ge(tp_done, s.tp + 2 * (k - 1) if k >= 2 else a["ukv"].tp + 8)
                evac(s.item + k, k % 2, u[:, k % 2, :, 0:384], src=gm[:, k % 2, :, 0:384])
            for h in range(MH + 2):
                if h < MH:
                    act.wait_ge(s_made, h + 1)
                    for b, (c0, c1) in enumerate(((0, 1), (1, 3))):
                        if h >= 2:
                            act.wait_ge(tp_done, a["heads"].tp + h - 1)
                        k = 4 * (h % 2) + b
                        act.activation(probs[:, h % 2, c0:c1, :], sc[:, c0:c1, :], ACT.Exp, scale=MSCALE,
                                       bias=stats[:, 2, k:k + 1],
                                       accum_out=stats[:, 2, k + 2:k + 3]).then_inc(p_made, 1)
                if h >= 2:
                    act.wait_ge(ms_done, made(head_fill(h - 2, True)))
                    act.activation(o_hi[:, h - 2, :], ms[:, head_fill(h - 2, True) % 2, 0:T],
                                   ACT.Copy).then_inc(o_split, 1)
            add_section("mla_out")
            act.wait_ge(x_added, added["down10"])
            squares("norm5", x_sb, xn)
            normalised("norm5")
            act.wait_ge(columns_on, 5)
            split(a["norm5"].tp, 8, (h_hi,), (ab[:, A_OF["ffn1"]],), (ab[:, A_OF["ffn1"] + 1],))
            for g in range(3):
                up(1, g)
                down(1, g)
            act.wait_ge(x_added, added["end"])
            squares("final", x_sb, y_out)

        @block.vector
        def _(dve):
            a = at
            step = Steps(dve, dve_step)

            def lo(n, slot=None):
                if isinstance(n, int) and n >= TOTAL:
                    return
                k, words = n if slot is None else slot, words_of(n)
                dve.wait_ge(hi_made, n + 1)
                dve.tensor_tensor(w_lo[:, k % RAW, 0:words], raw[:, k % RAW, 0:words],
                                  w_hi[:, k % RAW, 0:words].bitcast(F32), ALU.subtract).then_inc(lo_made, 1)

            def mod(n, slot, g, kt):
                dve.wait_ge(mod_in[slot], 16 * ((n - FIRST) // MODS + 1) if isinstance(n, int)
                            else 8 * (n - FIRST - slot) + 16)
                dve.wait_ge(mod_used, n)
                ck = c_col[:, kt:kt + 1] if isinstance(kt, int) else c_col[:, bass.ds(kt, 1)]
                dve.scalar_tensor_tensor(acc[:, g % 2, :], mods[:, slot, :], ck, acc[:, g % 2, :],
                                         ALU.mult, ALU.add).then_inc(mod_used, 1)

            def gate_row(g, j):
                fill = reduce_at(g) + j
                if j == 0:
                    dve.wait_ge(gate_in, 16 * (GATES.index(g) + 1))
                dve.wait_ge(ms_done, made(fill))
                v = gate_b[:, j * W:(j + 1) * W]
                dve.scalar_tensor_tensor(v, ms[:, fill % 2, :], 1.0, v, ALU.add, ALU.add).then_inc(ms_free, 1)

            def reduced(g):
                fill = reduce_at(g)
                if g in GATES:
                    for j in range(4):
                        gate_row(g, j)
                    dve.wait_ge(ms_free, fill + 4)
                else:
                    tile_, col = mod_bias(g)
                    bias = pcol[:, tile_, col:col + KT]
                    dve.wait_ge(ms_done, made(fill))
                    psum = ms[:, fill % 2, 0:KT]
                    if g in SHIFT:
                        dve.tensor_tensor(ab[:, A_OF[SHIFT[g][0]] + 1, :], psum, bias, ALU.add).then_inc(ms_free, 1)
                        dve.wait_ge(ms_free, fill + 1)
                    else:
                        norm, gain = SCALE[g]
                        dve.tensor_tensor(modc[:, 0, :], psum, bias, ALU.add).then_inc(ms_free, 1)
                        dve.wait_ge(ms_free, fill + 1)
                        dve.scalar_tensor_tensor(ab[:, A_OF[norm], :], modc[:, 0, :], 1.0,
                                                 pcol[:, 0, gain:gain + KT], ALU.add,
                                                 ALU.mult).then_inc(columns_on, 1)
                        dve.wait_ge(columns_on, list(SCALE).index(g) + 1)

            def split(name, count, dst, hi_of, scale, shift):
                fill = a[name].tp
                for f in range(count):
                    dve.wait_ge(split_hi, splits[name] + f + 1)
                    for m, (d, h_, sc_, sh_) in enumerate(zip(dst, hi_of, scale, shift)):
                        for k in range(2):
                            kt = 2 * f + k
                            t = tp[:, (fill + f) % 2, k * T:(k + 1) * T]
                            if sh_ is None:
                                ins = dve.tensor_scalar(both[:, k, :], t, sc_[:, kt:kt + 1], None, ALU.mult)
                            else:
                                ins = dve.tensor_scalar(both[:, k, :], t, sc_[:, kt:kt + 1], sh_[:, kt:kt + 1],
                                                        ALU.mult, ALU.add)
                            v = step.mark(ins)
                        step.wait(v)
                        ins = dve.tensor_tensor(d[:, 2 * f:2 * f + 2, :], both[:, :, :],
                                                h_[:, 2 * f:2 * f + 2, :].bitcast(F32), ALU.subtract)
                        if m == len(dst) - 1:
                            ins.then_inc(tp_free, 1)
                        else:
                            step.link(ins)
                    dve.wait_ge(tp_free, fill + f + 1)

            def normalised(name, src, dst, tiles=1):
                dve.wait_ge(rstd, NORM[name] + 1)
                for t in range(tiles):
                    k = TT * (NORM[name] % 2) + t
                    dve.tensor_scalar(dst[:, t, :], src[:, t, :], stats[:, 1, k:k + 1], None,
                                      ALU.mult).then_inc(xn_made, 1)

            def add_chunk(chunk, par, cols):
                dve.wait_ge(u_made, chunk + 1)
                g = gate_b[:, cols].rearrange("p (o n) -> p o n", o=1).to_broadcast([P, TT, W])
                step.link(dve.tensor_tensor(u[:, par], u[:, par], g, ALU.mult))
                dve.tensor_tensor(x_sb[:, :, cols], x_sb[:, :, cols], u[:, par], ALU.add).then_inc(x_added, 1)

            def section(name, group, mods_per, extra=None, kt0=0):
                s = a[name]
                dve.wait_ge(acc_zero, group + 1)
                links = {None: 0, "add": 2}[extra]
                with dve.Fori(0, s.n) as i, step.loop(i, 0, s.n, links):
                    for k in range(8):
                        if extra == "add" and k == 7:
                            add_chunk(s.chunk + 2 * i + 1, 1, bass.ds(1024 * i + W, W))
                        mk = k - (8 - mods_per)
                        if mk >= 0:
                            mod(s.mod + mods_per * i + mk, mk % MODS, group, kt0 + mods_per * i + mk)
                        lo(s.item + AHEAD + 8 * i + k, s.item + AHEAD + k)
                        if extra == "add" and k == 3:
                            par = k // 4
                            add_chunk(s.chunk + 2 * i + par, par, bass.ds(1024 * i + par * W, W))

            def evac_tp(fill, dst, src, scale=None):
                dve.wait_ge(tp_done, fill + 1)
                if scale is None:
                    dve.tensor_copy(dst, src).then_inc(tp_free, 1)
                else:
                    dve.tensor_scalar(dst, src, scale, None, ALU.mult).then_inc(tp_free, 1)

            dve.wait_ge(consts, 1)
            dve.wait_ge(rows_in, 16 * 19)
            step.link(dve.tensor_copy(pos_f[:, :], pos_i[:, :]))
            for t in range(TT):
                step.link(dve.tensor_scalar(ang[:, 2, t, :], inv[:, :], pos_f[:, t:t + 1], None, ALU.mult))
            step.link(dve.tensor_scalar(ang[:, 1], ang[:, 2], 1.0 / TWO_PI, ROUND, ALU.mult, ALU.add))
            step.link(dve.tensor_scalar(ang[:, 1], ang[:, 1], -ROUND, None, ALU.add))
            for part in (*SPLIT_2PI, TWO_PI - sum(SPLIT_2PI)):
                step.link(dve.scalar_tensor_tensor(ang[:, 2], ang[:, 1], -part, ang[:, 2], ALU.mult, ALU.add))
            step.link(dve.tensor_scalar(ang[:, 0], ang[:, 2], 3.1415925, -3.1415925, ALU.min, ALU.max))
            dve.tensor_scalar(ang[:, 1], ang[:, 0], 0.5, None, ALU.mult).then_inc(ang_made, 1)
            s = a["setup"]
            dve.wait_ge(tp_done, 1)
            for t, rows in enumerate((104, P, 96)):
                step.mark(dve.tensor_copy(pcol[:, t, 0:rows], tp[:, 0, t * P:t * P + rows]))
            dve.tensor_copy(c_col[:, :], tp[:, 0, 3 * P:3 * P + KT]).then_inc(tp_free, 1)
            for layer in range(2):
                evac_tp(1 + layer, cv_col[:, layer], tp[:, (1 + layer) % 2, 0:8 * FT].rearrange("p (k c) -> p k c", k=4))
            dve.wait_ge(tp_free, 3)
            dve.wait_ge(sin_made, 2)
            step.link(dve.tensor_tensor(cos[:, :, :], cos[:, :, :], cos[:, :, :], ALU.mult))
            step.link(dve.tensor_scalar(cos[:, :, :], cos[:, :, :], -2.0, 1.0, ALU.mult, ALU.add))
            dve.wait_ge(acc_zero, 2)
            for n in range(FIRST):
                if n == KT:
                    normalised("norm0", x_sb, xn)
                ring, g = MODS + RAW, n // KT
                dve.wait_ge(first_in[n % ring], 16 * (n // ring + 1))
                if n:
                    dve.wait_ge(mod_used, n)
                dve.scalar_tensor_tensor(acc[:, g, :], first_slot(n), c_col[:, n % KT:n % KT + 1], acc[:, g, :],
                                         ALU.mult, ALU.add).then_inc(mod_used, 1)
            reduced(0)
            reduced(1)
            split("norm0", 8, (h_lo,), (h_hi,), (ab[:, A_OF["mix0"]],), (ab[:, A_OF["mix0"] + 1],))
            for n in range(AHEAD):
                lo(n)
            s = a["gate"]
            dve.wait_ge(item_used, s.item + 1)
            dve.tensor_copy(g1_t[0:RANK, :], ms[0:RANK, s.ms % 2, 0:T]).then_inc(ms_free, 1)
            lo(AHEAD)

            def log_decays(f):
                s = a["gate"]
                t, half = f // 2, f % 2
                v = la[:, t, half * W:(half + 1) * W]
                dve.wait_ge(z_log, f + 1)
                dve.scalar_tensor_tensor(v, ms[:, (s.ms + 1 + f) % 2, :], 0.0, v, ALU.min,
                                         ALU.subtract).then_inc(ms_free, 1)

            def decay_sums(f):
                s = a["gate"]
                t, half = f // 2, f % 2
                dve.wait_ge(ms_done, made(s.ms + 5 + f))
                dve.tensor_copy(b_sb[:, 4 * half:4 * half + 4, t * P:(t + 1) * P],
                                ms[:, (s.ms + 5 + f) % 2, :].rearrange("p (k i) -> p k i", k=4)).then_inc(ms_free, 1)

            s = a["qk"]
            dve.wait_ge(acc_zero, 3)

            def turned(fill, j, i):
                tile_ = DKT * i + 2 * j
                dst = qk_t[:, tile_:tile_ + 2, :] if isinstance(tile_, int) else qk_t[:, bass.ds(tile_, 2), :]
                evac_tp(fill, dst, tp[:, (s.tp + j) % 2, :].rearrange("p (k t) -> p k t", k=2), 0.25)

            def qk_body(i, turn):
                for k in range(8):
                    mod(s.mod + 8 * i + k, k % MODS, 2, 8 * i + k)
                    lo(s.item + AHEAD + 8 * i + k)
                    if i == 0 and k in (1, 2):
                        log_decays(2 * k - 2)
                        log_decays(2 * k - 1)
                    if i == 0 and k == 3:
                        for f in range(4):
                            decay_sums(f)
                    if turn and k < 4:
                        turned(s.tp + 4 * (i - 1) + k, k, i - 1)

            qk_body(0, False)
            qk_body(1, True)
            for k in range(4):
                turned(s.tp + 4 + k, k, 1)
            s = a["diag"]
            step.link(dve.memset(st[:, :, :, :], 0.0))
            dve.wait_ge(consts, 2)

            def pick(fill, level, hh):
                dve.wait_ge(ms_done, made(fill))
                dve.copy_predicated(
                    st[:, 2 * hh:2 * hh + 2, :, :].rearrange("p h t i -> p (h t) i"),
                    mask[:, level:level + 1, :].to_broadcast([P, 4, P]),
                    ms[:, fill % 2, :].rearrange("p (k i) -> p k i", k=4)).then_inc(ms_free, 1)

            for hh in range(2):
                pick(s.ms + hh, 7, hh)

            def exponents(n):
                w, hh = UNITS[n]
                b = b_sb[:, 4 * hh:4 * hh + 4, :]
                first, second = halves(b, w, 0), halves(b, w, 1)
                middle = first[:, :, w - 1:w].to_broadcast([P, 4 * T // (2 * w), w])
                if n >= 2:
                    dve.wait_ge(ms_done, made(a["v"].ms + n - 2))
                step.mark(dve.tensor_tensor(halves(ex[:, n % 2], w, 0), middle, first, ALU.subtract))
                if w == P:
                    dve.tensor_copy(halves(ex[:, n % 2], w, 1), second).then_inc(e_made, 1)
                else:
                    dve.tensor_tensor(halves(ex[:, n % 2], w, 1), second, middle, ALU.subtract).then_inc(e_made, 1)

            def picked(n):
                w, hh = UNITS[n]
                fill = a["v"].ms + n
                if w == P:
                    dve.wait_ge(ms_done, made(fill))
                    dve.tensor_copy(sx[:, 2 * hh:2 * hh + 2, :],
                                    ms[:, fill % 2, 0:2 * P].rearrange("p (h i) -> p h i", h=2)).then_inc(ms_free, 1)
                else:
                    pick(fill, LEVELS.index(w), hh)

            s = a["v"]
            dve.wait_ge(ms_free, a["gate"].ms + 9)
            dve.wait_ge(acc_zero, 4)
            for k in range(16):
                exponents(k)
                mod(s.mod + k, k % MODS, 3, k)
                lo(s.item + AHEAD + k)
                if k:
                    dve.wait_ge(ms_free, s.ms + k - 1)
                    picked(k - 1)
            dve.wait_ge(ms_free, s.ms + 15)
            picked(15)
            reduced(2)
            reduced(3)
            section("r", 4, 4)
            for h in range(HEADS):
                dve.wait_ge(o_rstd, h + 1)
                for t in range(TT):
                    v = r_sb[:, t, h * DV:(h + 1) * DV]
                    ins = dve.scalar_tensor_tensor(v, gm[:, h % 2, t, :], stats[:, 1, TT * h + t:TT * h + t + 1],
                                                   v, ALU.mult, ALU.mult)
                    step.mark(ins) if t == 0 else ins.then_inc(o_gated, 1)
            split("o", 8, (h_lo,), (h_hi,), (pcol[:, 0, HEAD:HEAD + KT],), (None,))
            dve.wait_ge(x_in, 32)
            section("gla_out", 4, 4, "add", kt0=8)
            reduced(4)
            dve.wait_ge(x_added, 4)
            normalised("norm1", x_sb, xn)
            split("norm1", 8, (h_lo,), (h_hi,), (ab[:, A_OF["ffn0"]],), (ab[:, A_OF["ffn0"] + 1],))

            def conv_tile(layer, g, blk, j, fill, tile_):
                bank = (a[f"up{layer}{g}"].tp + j) % 2
                ft = sum(UP_BLOCKS[:g]) * 4 + j
                dve.wait_ge(taps, tile_ + 1)
                for tap, shift in ((1, 1), (0, 2)):
                    for side in (1, 0):
                        col = 4 * blk + (ft + side * FT)
                        cs = slice(col, col + 1) if isinstance(col, int) else bass.ds(col, 1)
                        v = conv[:, j % 2, side, shift:T]
                        ins = dve.scalar_tensor_tensor(v, tp[:, bank, side * T:(side + 1) * T - shift],
                                                       cv_col[:, layer, tap, cs], v, ALU.mult, ALU.add)
                        if tap:
                            last = step.mark(ins)
                        elif side:
                            ins.then_inc(conv_made, 1)
                        else:
                            ins.then_inc(tp_free, 1)
                    if tap:
                        step.wait(last)

            def conv_product(j, fill, tile_):
                dve.wait_ge(silu_made, tile_ + 1)
                dve.wait_ge(tp_free, fill + 1)
                dve.tensor_tensor(gated[:, j % 2, :], conv[:, j % 2, 0, :], conv[:, j % 2, 1, :],
                                  ALU.mult).then_inc(gated_made, 1)

            def conv_lo(blk, j, tile_):
                dve.wait_ge(act_hi, tile_ + 1)
                kt = 4 * blk + j
                ks = slice(kt, kt + 1) if isinstance(kt, int) else bass.ds(kt, 1)
                dve.tensor_tensor(a_lo[:, ks, :], gated[:, j % 2:j % 2 + 1, :],
                                  a_hi[:, ks, :].bitcast(F32), ALU.subtract).then_inc(act_lo, 1)

            def up(layer, g, group, mods_per, before=None):
                s = a[f"up{layer}{g}"]
                t0 = ffn_tiles[f"up{layer}{g}"]
                if mods_per:
                    dve.wait_ge(acc_zero, group + 1)

                bare = up_bare(mods_per, s.n)

                def body(i, conv_too, mods_per=mods_per):
                    for k in range(8):
                        mk = k - (8 - mods_per)
                        if mk >= 0:
                            m = mods_per * (i - bare) + mk
                            mod(s.mod + m, mk % MODS, group, m)
                        tile_, fill = t0 + 4 * (i - 1) + k, s.tp + 4 * (i - 1) + k
                        if conv_too and k < 4:
                            conv_tile(layer, g, i - 1, k, fill, tile_)
                        if conv_too and 1 <= k <= 4:
                            conv_product(k - 1, fill - 1, tile_ - 1)
                        lo(s.item + AHEAD + 8 * i + k, s.item + AHEAD + k)
                        if before is not None and not conv_too and k == 2:
                            reduced(before)
                        if conv_too and 1 <= k <= 4:
                            conv_lo(i - 1, k - 1, tile_ - 1)

                body(0, False, 0 if bare else mods_per)
                assert bare <= 1
                if g == 2:
                    for i in range(1, s.n):
                        body(i, True)
                else:
                    with dve.Fori(1, s.n) as i, step.loop(i, 1, s.n, 8):
                        body(i, True)

            def down(layer, g, up_group, group):
                s, u_, n = a[f"down{layer}{g}"], a[f"up{layer}{g}"], UP_BLOCKS[g] - 1
                tile0, fill0 = ffn_tiles[f"up{layer}{g}"] + 4 * n, u_.tp + 4 * n
                if group is not None:
                    dve.wait_ge(acc_zero, group + 1)

                def last_tiles(first):
                    for j in (first, first + 1):
                        conv_tile(layer, g, n, j, fill0 + j, tile0 + j)
                    for j in (first, first + 1):
                        dve.wait_ge(act_lo, tile0 + j - 1)
                        conv_product(j, fill0 + j, tile0 + j)
                    for j in (first, first + 1):
                        conv_lo(n, j, tile0 + j)

                for k in range(16):
                    if k == 1:
                        last_tiles(2)
                    if k == 15:
                        add_chunk(s.chunk + 3, 1, slice(3 * W, 4 * W))
                    if group is not None:
                        mod(s.mod + k, k % MODS, group, k)
                    lo(s.item + AHEAD + k)
                    if k == 0:
                        last_tiles(0)
                    if up_group in GATES:
                        if 3 <= k < 7:
                            gate_row(up_group, k - 3)
                        if k == 6:
                            dve.wait_ge(ms_free, reduce_at(up_group) + 4)
                            add_chunk(s.chunk, 0, slice(0, W))
                    elif k == 2 and up_group is not None:
                        reduced(up_group)
                    if k % 4 == 3 and k < 15 and not (k == 3 and up_group in GATES):
                        ch = k // 4
                        add_chunk(s.chunk + ch, ch % 2, slice(ch * W, (ch + 1) * W))

            for g, (ug, um, dg) in enumerate(((5, 4, 6), (7, 4, 8), (9, 8, 10))):
                up(0, g, ug, um, (None, 6, 8)[g])
                down(0, g, ug, dg)

            dve.wait_ge(x_added, added["mla_out"])
            normalised("norm2", x_sb, xn)
            split("norm2", 8, (h_lo, a_lo), (h_hi, a_hi), (ab[:, A_OF["mix1"]], ab[:, A_OF["kv"]]),
                  (ab[:, A_OF["mix1"] + 1], ab[:, A_OF["kv"] + 1]))
            s = a["latent"]
            for k in range(9):
                lo(s.item + AHEAD + k)
                if k == 4:
                    reduced(10)

            def rotate(x1, x2, out1, out2, n):
                cb = cos[:, :, :].rearrange("p t (o r) -> p t o r", o=1).to_broadcast([P, TT, n, HR])
                sb_ = sin[:, :, :].rearrange("p t (o r) -> p t o r", o=1).to_broadcast([P, TT, n, HR])
                for k, (v, w_) in enumerate(((x1, cb), (x2, sb_), (x2, cb), (x1, sb_))):
                    last = step.mark(dve.tensor_tensor(rt[:, k, :, 0:n, :], v, w_, ALU.mult))
                step.wait(last)
                step.mark(dve.tensor_tensor(out1, rt[:, 0, :, 0:n, :], rt[:, 1, :, 0:n, :], ALU.subtract))
                return dve.tensor_tensor(out2, rt[:, 2, :, 0:n, :], rt[:, 3, :, 0:n, :], ALU.add)

            normalised("norm3", u[:, 0], u[:, 0], TT)
            normalised("norm4", u[:, 1], u[:, 1], TT)
            dve.wait_ge(item_used, s.item + 9)
            kv = ms[:, s.ms % 2, 0:TT * ROPE].rearrange("p (t o r) -> p t o r", t=TT, o=1)
            ins = rotate(kv[:, :, :, 0:HR], kv[:, :, :, HR:ROPE], kr[:, :, 0:1, 0:HR], kr[:, :, 0:1, HR:ROPE], 1)
            ins.then_inc(ms_free, 1)
            dve.wait_ge(ms_free, s.ms + 1)
            dve.tensor_copy(kr[:, :, 1, :], kr[:, :, 0, :]).then_inc(roped, 1)
            split("norm3", 2, (ckv_lo,), (ckv_hi,), (pcol[:, 0, KVL:KVL + LT],), (None,))
            split("norm4", 2, (cq_lo,), (cq_hi,), (pcol[:, 0, QL:QL + LT],), (None,))
            evac_tp(a["krope"].tp, kr_t[:, :], tp[:, a["krope"].tp % 2, 0:T])

            s = a["ukv"]
            dve.wait_ge(acc_zero, 12)

            def keys(k):
                evac_tp(s.tp + k, k_t[:, 2 * k:2 * k + 2, :],
                        tp[:, (s.tp + k) % 2, :].rearrange("p (h t) -> p h t", h=2))

            for k in range(8):
                mod(s.mod + k, k % MODS, 11, k)
                lo(s.item + AHEAD + k)
                if k:
                    keys(k - 1)
            keys(7)
            q = a["uq"]

            def queries(k):
                f = q.tp + 2 * k
                evac_tp(f, q_t[:, 2 * k:2 * k + 2, :], tp[:, f % 2, :].rearrange("p (h t) -> p h t", h=2))
                evac_tp(f + 1, qr_t[:, k, :], tp[:, (f + 1) % 2, 0:T])

            for k in range(8):
                mod(q.mod + k, k % MODS, 11, 8 + k)
                lo(q.item + AHEAD + k)
                if k:
                    queries(k - 1)
                dve.wait_ge(u_made, q.chunk + k + 1)
                v = u[:, k % 2, :, 0:384].rearrange("p t (h c) -> p t h c", h=2)
                rotate(v[:, :, :, P:P + HR], v[:, :, :, P + HR:P + ROPE],
                       qr[:, :, :, 0:HR], qr[:, :, :, HR:ROPE], 2).then_inc(roped, 1)
            queries(7)
            reduced(11)
            f = a["heads"]
            dve.wait_ge(consts, 3)
            for h in range(MH + 2):
                if 1 <= h <= MH:
                    pr = probs[:, (h - 1) % 2]
                    k = 4 * ((h - 1) % 2)
                    dve.wait_ge(p_made, 2 * h)
                    step.link(dve.reciprocal(stats[:, 2, 8:10], stats[:, 2, k + 2:k + 4]))
                    step.mark(dve.tensor_scalar(pr[:, 0, :], pr[:, 0, :], stats[:, 2, 8:9], None, ALU.mult))
                    dve.tensor_scalar(pr[:, 1:3, :], pr[:, 1:3, :], stats[:, 2, 9:10], None,
                                      ALU.mult).then_inc(p_norm, 1)
                if h < MH:
                    fill = head_fill(h, False)
                    dve.wait_ge(ms_done, made(fill))
                    dve.tensor_tensor(sc[:, :, :], ms[:, fill % 2, 0:3 * P].rearrange("p (b k) -> p b k", b=3),
                                      causal[:, :, :], ALU.add).then_inc(ms_free, 1)
                    dve.wait_ge(ms_free, fill + 1)
                    step.mark(dve.reduce_max(stats[:, 2, 10:11], sc[:, 0, :], AX_X))
                    step.link(dve.reduce_max(stats[:, 2, 11:12], sc[:, 1:3, :].rearrange("p a b -> p (a b)"), AX_X))
                    k = 4 * (h % 2)
                    dve.tensor_scalar(stats[:, 2, k:k + 2], stats[:, 2, 10:12], -MSCALE, None,
                                      ALU.mult).then_inc(s_made, 1)
                if 1 <= h <= MH:
                    t = f.tp + h - 1
                    dve.wait_ge(tp_done, t + 1)
                    if h >= 2:
                        dve.wait_ge(ms_done, made(head_fill(h - 2, True)))
                    dve.tensor_copy(p_t[:, :, :], tp[:, t % 2, 0:3 * P].rearrange("p (b k) -> p b k", b=3))\
                       .then_inc(tp_free, 1)
                if h >= 2:
                    fill = head_fill(h - 2, True)
                    dve.wait_ge(o_split, h - 1)
                    dve.tensor_tensor(o_lo[:, h - 2, :], ms[:, fill % 2, 0:T], o_hi[:, h - 2, :].bitcast(F32),
                                      ALU.subtract).then_inc(ms_free, 1)
            section("mla_out", 12, 8, "add")
            reduced(12)
            dve.wait_ge(x_added, added["down10"])
            normalised("norm5", x_sb, xn)
            split("norm5", 8, (h_lo,), (h_hi,), (ab[:, A_OF["ffn1"]],), (ab[:, A_OF["ffn1"] + 1],))
            for g in range(3):
                up(1, g, 13 if g == 0 else None, 4 if g == 0 else 0)
                down(1, g, 13 if g == 0 else None, None)
            dve.wait_ge(gate_in, 16 * 5)
            dve.wait_ge(rstd, NORM["final"] + 1)
            for t in range(TT):
                k = TT * (NORM["final"] % 2) + t
                dve.scalar_tensor_tensor(y_out[:, t, :], x_sb[:, t, :], stats[:, 1, k:k + 1], gate_b[:, :],
                                         ALU.mult, ALU.mult).then_inc(xn_made, 1)

        @block.tensor
        def _(pe):
            a = at

            def item(n, slot, hi_s, lo_s, par, q, k_tiles=KT_ITEM, width=W, total=KT):
                pe.wait_ge(lo_made, n + 1)
                wh = w_hi[:, slot % RAW, 0:k_tiles * width].rearrange("p (j n) -> p j n", j=k_tiles)
                wl = w_lo[:, slot % RAW, 0:k_tiles * width].rearrange("p (j n) -> p j n", j=k_tiles)
                for j in range(k_tiles):
                    kt = q * k_tiles + j
                    for t in range(TT):
                        o, tok = gm[:, par, t, 0:width], slice(t * P, (t + 1) * P)
                        pe.matmul(o, hi_s[:, kt, tok], wh[:, j, :], start=kt == 0, stop=False)
                        pe.matmul(o, hi_s[:, kt, tok], wl[:, j, :], start=False, stop=False)
                        ins = pe.matmul(o, lo_s[:, kt, tok], wh[:, j, :], start=False, stop=kt == total - 1)
                ins.then_inc(item_used, 1)

            def gm_free(chunk):
                if not (isinstance(chunk, int) and chunk < 2):
                    pe.wait_ge(u_made, chunk - 1)

            def transposes(fill, bank, parts):
                if not (isinstance(fill, int) and fill < 2):
                    pe.wait_ge(tp_free, fill - 1)
                for src, col in parts:
                    k, m = src.shape[0], src.shape[1]
                    ins = pe.transpose(tp[0:m, bank, col:col + k], src, ident[0:k, 0:k])
                ins.then_inc(tp_done, 1)

            def ms_open(fill):
                if fill >= 2:
                    pe.wait_ge(ms_free, fill - 1)
                return ms[:, fill % 2, :]

            def narrow(n, fill, hi_s, lo_s, width):
                pe.wait_ge(lo_made, n + 1)
                o = ms_open(fill)
                wh = w_hi[:, n % RAW, 0:KT * width].rearrange("p (j n) -> p j n", j=KT)
                wl = w_lo[:, n % RAW, 0:KT * width].rearrange("p (j n) -> p j n", j=KT)
                for t in range(TT):
                    v, tok = o[:, t * width:(t + 1) * width], slice(t * P, (t + 1) * P)
                    for kt in range(KT):
                        pe.matmul(v, hi_s[:, kt, tok], wh[:, kt, :], start=kt == 0, stop=False)
                        pe.matmul(v, hi_s[:, kt, tok], wl[:, kt, :], start=False, stop=False)
                        ins = pe.matmul(v, lo_s[:, kt, tok], wh[:, kt, :], start=False, stop=kt == KT - 1)
                ins.then_inc(item_used, 1)

            def reduce_mod(g, parts=range(4)):
                name = REDUCE[g][0]
                pe.wait_ge(mod_used, KT * (g + 1))
                fill = reduce_at(g)
                if g in GATES:
                    for j in parts:
                        o = ms_open(fill + j)
                        pe.matmul(o, ones[:, :], acc[:, g % 2, j * W:(j + 1) * W],
                                  start=True, stop=True).then_inc(ms_done, 1)
                else:
                    o = ms_open(fill)
                    for j in range(KT):
                        ins = pe.matmul(o[:, j:j + 1], acc[:, g % 2, j * P:(j + 1) * P], ones[:, 0:1],
                                        start=True, stop=True)
                    ins.then_inc(ms_done, 1)

            def turn_rows(name, fills, tile_of):
                s = a[name]
                for f in fills:
                    transposes(s.tp + f, (s.tp + f) % 2,
                               [(tile_of(2 * f + k, t), k * T + t * P) for k in range(2) for t in range(TT)])

            def turn_wide(name, q, src=xn):
                if q == 0 and name in NORM:
                    pe.wait_ge(xn_made, TT * (NORM[name] + 1))
                ahead = [0, 4, 6, 8, 8]
                turn_rows(name, range(ahead[q], ahead[q + 1]), lambda kt, t: src[:, t, kt * P:(kt + 1) * P])
                pe.wait_ge(tp_free, a[name].tp + 2 * (q + 1))

            def section(name, hi_s, lo_s, turned=None):
                s = a[name]

                def body(i, turned=None):
                    for k in range(8):
                        if k % 4 == 0:
                            gm_free(s.chunk + 2 * i + k // 4)
                        if turned and k < 4:
                            turn_wide(turned, k, r_sb)
                        item(s.item + 8 * i + k, s.item + k, hi_s, lo_s, k // 4, k % 4)

                if turned:
                    body(0, turned)
                with pe.Fori(1 if turned else 0, s.n) as i:
                    body(i)

            pe.wait_ge(consts, 1)
            pe.wait_ge(rows_in, 16 * 19)
            pe.wait_ge(c_act_made, 1)
            transposes(0, 0, [(prow[0:104, 0, :], 0), (prow[:, 1, :], P), (prow[0:96, 2, :], 2 * P),
                              (crow[:, 1, :], 3 * P)])
            for layer in range(2):
                transposes(1 + layer, (1 + layer) % 2,
                           [(cvrow[:, 4 * layer + k, :], 2 * FT * k) for k in range(4)])
            reduce_mod(0)
            reduce_mod(1)
            for q in range(4):
                turn_wide("norm0", q)

            def gate_step(k):
                s = a["gate"]
                if k in (1, 2):
                    if k == 1:
                        pe.wait_ge(ms_free, s.ms + 1)
                        pe.wait_ge(wg_in, 32)
                    for f in (0, 1) if k == 1 else (2, 3):
                        t, half = f // 2, f % 2
                        pe.matmul(ms_open(s.ms + 1 + f), g1_t[0:RANK + 1, t * P:(t + 1) * P],
                                  wg2[:, half * W:(half + 1) * W], start=True, stop=True).then_inc(ms_done, 1)
                if k == 3:
                    for f in range(4):
                        t, half = f // 2, f % 2
                        pe.wait_ge(ms_free, s.ms + 1 + f + 1)
                        o = ms_open(s.ms + 5 + f)
                        for j in range(4):
                            c0 = (4 * half + j) * P
                            ins = pe.matmul(o[:, j * P:(j + 1) * P], la[:, t, c0:c0 + P], tri[:, :],
                                            start=True, stop=True)
                        ins.then_inc(ms_done, 1)

            s = a["gate"]
            pe.wait_ge(lo_made, s.item + 1)
            wh = w_hi[:, s.item % RAW, 0:KT * RANK].rearrange("p (j n) -> p j n", j=KT)
            wl = w_lo[:, s.item % RAW, 0:KT * RANK].rearrange("p (j n) -> p j n", j=KT)
            o = ms_open(s.ms)[0:RANK, 0:T]
            for kt in range(KT):
                pe.matmul(o, wh[:, kt, :], h_hi[:, kt, :], start=kt == 0, stop=False)
                pe.matmul(o, wh[:, kt, :], h_lo[:, kt, :], start=False, stop=False)
                ins = pe.matmul(o, wl[:, kt, :], h_hi[:, kt, :], start=False, stop=kt == KT - 1)
            ins.then_inc(item_used, 1)

            s = a["qk"]

            def turn_qk(i, f):
                pe.wait_ge(u_made, s.chunk + 2 * i + f // 2 + 1)
                transposes(s.tp + 4 * i + f, (s.tp + f) % 2,
                           [(u[:, f // 2, t, (2 * (f % 2) + k) * P:(2 * (f % 2) + k + 1) * P], k * T + t * P)
                            for k in range(2) for t in range(TT)])

            for i in range(2):
                for k in range(8):
                    if k % 4 == 0:
                        gm_free(s.chunk + 2 * i + k // 4)
                    item(s.item + 8 * i + k, s.item + k, h_hi, h_lo, k // 4, k % 4)
                    if i == 0:
                        gate_step(k)
                    if i and k < 4:
                        turn_qk(i - 1, k)
            for f in range(4):
                turn_qk(1, f)
            pe.wait_ge(tp_free, s.tp + 8)
            s = a["diag"]
            for hh in range(2):
                o = ms_open(s.ms + hh)
                for hl in range(2):
                    for t in range(TT):
                        c0, tok = (2 * hl + t) * P, slice(t * P, (t + 1) * P)
                        for d in range(2):
                            k = 4 * hh + 2 * hl + d
                            ins = pe.matmul(o[:, c0:c0 + P], qk_t[:, DKT + k, tok], qk_t[:, k, tok],
                                            start=d == 0, stop=d == 1)
                ins.then_inc(ms_done, 1)

            def scores(n):
                w, hh = UNITS[n]
                pe.wait_ge(xq_made, 2 * n + 2)
                o = ms_open(a["v"].ms + n)
                for hl in range(2):
                    for t in range(1 if w == P else TT):
                        c0 = hl * P if w == P else (2 * hl + t) * P
                        for d in range(2):
                            e = ex[:, n % 2, 2 * hl + d, :]
                            key, query = (e[:, 0:P], e[:, P:T]) if w == P else (e[:, t * P:(t + 1) * P],) * 2
                            ins = pe.matmul(o[:, c0:c0 + P], key, query, start=d == 0, stop=d == 1)
                ins.then_inc(ms_done, 1)

            s = a["v"]
            for k in range(16):
                if k % 4 == 0:
                    gm_free(s.chunk + k // 4)
                item(s.item + k, s.item + k, h_hi, h_lo, (k // 4) % 2, k % 4)
                if k:
                    scores(k - 1)
            scores(15)
            reduce_mod(2)
            reduce_mod(3)
            section("r", h_hi, h_lo)
            pe.wait_ge(ms_free, a["v"].ms + 16)
            for h in range(HEADS):
                if h < 2:
                    gm_free(a["gla_out"].chunk + h)
                else:
                    pe.wait_ge(o_gated, h - 1)
                v0, v1 = v_sb[:, 0, h * DV:(h + 1) * DV], v_sb[:, 1, h * DV:(h + 1) * DV]
                pe.matmul(gm[:, h % 2, 0, :], st[:, h, 0, :], v0, start=True, stop=True)
                pe.matmul(gm[:, h % 2, 1, :], sx[:, h, :], v0, start=True, stop=False)
                pe.matmul(gm[:, h % 2, 1, :], st[:, h, 1, :], v1, start=False, stop=True).then_inc(o_ready, 1)
            pe.wait_ge(o_gated, HEADS)
            section("gla_out", h_hi, h_lo, "o")
            reduce_mod(4)

            def turn_pair(layer, g, i, j):
                s = a[f"up{layer}{g}"]
                transposes(s.tp + 4 * i + j, (s.tp + j) % 2,
                           [(u[:, side, t, j * P:(j + 1) * P], side * T + t * P)
                            for side in range(2) for t in range(TT)])

            def ffn(layer, norm, up_groups, down_groups):
                for g, blocks in enumerate(UP_BLOCKS):
                    s = a[f"up{layer}{g}"]

                    def block_(i, turn):
                        for k in range(8):
                            if k % 4 == 0:
                                gm_free(s.chunk + 2 * i + k // 4)
                            if g == 0 and not turn and k < 4:
                                turn_wide(norm, k)
                            item(s.item + 8 * i + k, s.item + k, h_hi, h_lo, k // 4, k % 4)
                            if g and not turn and k == 2 and down_groups[g - 1] is not None:
                                reduce_mod(down_groups[g - 1])
                            if turn and k < 4:
                                if k == 0:
                                    pe.wait_ge(u_made, s.chunk + 2 * i)
                                turn_pair(layer, g, i - 1, k)

                    block_(0, False)
                    with pe.Fori(1, blocks) as i:
                        block_(i, True)
                    tiles = ffn_tiles[f"up{layer}{g}"]
                    s = a[f"down{layer}{g}"]
                    for k in range(16):
                        if k % 4 == 0:
                            gm_free(s.chunk + k // 4)
                        if k < 4:
                            pe.wait_ge(act_lo, tiles + blocks * (k + 1))
                        item(s.item + k, s.item + k, a_hi, a_lo, (k // 4) % 2, k % 4, k_tiles=blocks,
                             total=4 * blocks)
                        if k < 2:
                            pe.wait_ge(u_made, a[f"up{layer}{g}"].chunk + 2 * blocks)
                            turn_pair(layer, g, blocks - 1, 2 * k)
                            turn_pair(layer, g, blocks - 1, 2 * k + 1)
                        if up_groups[g] in GATES:
                            if 2 <= k < 6:
                                reduce_mod(up_groups[g], (k - 2,))
                        elif k == 2 and up_groups[g] is not None:
                            reduce_mod(up_groups[g])

            ffn(0, "norm1", (5, 7, 9), (6, 8, 10))

            s = a["latent"]
            for k in range(8):
                if k % 4 == 0:
                    gm_free(s.chunk + k // 4)
                if k < 4:
                    turn_wide("norm2", k)
                src = (a_hi, a_lo) if k < 4 else (h_hi, h_lo)
                item(s.item + k, s.item + k, *src, k // 4, k % 4)
                if k == 4:
                    reduce_mod(10)
            narrow(s.item + 8, s.ms, a_hi, a_lo, ROPE)
            for name, side in (("norm3", 0), ("norm4", 1)):
                pe.wait_ge(xn_made, TT * (NORM[name] + 1))
                turn_rows(name, range(2), lambda kt, t, side=side: u[:, side, t, kt * P:(kt + 1) * P])
            pe.wait_ge(roped, 1)
            fill = a["krope"].tp
            transposes(fill, fill % 2, [(kr[:, t].rearrange("p a b -> p (a b)"), t * P) for t in range(TT)])

            s = a["ukv"]
            pe.wait_ge(tp_free, a["norm4"].tp + 2)

            def turn_keys(k):
                pe.wait_ge(u_made, s.chunk + k + 1)
                transposes(s.tp + k, (s.tp + k) % 2,
                           [(u[:, k % 2, t, hl * P:(hl + 1) * P], hl * T + t * P)
                            for hl in range(2) for t in range(TT)])

            for k in range(8):
                gm_free(s.chunk + k)
                item(s.item + k, s.item + k, ckv_hi, ckv_lo, k % 2, 0, total=LT)
                if k:
                    turn_keys(k - 1)
            turn_keys(7)
            q = a["uq"]

            def turn_queries(k):
                pe.wait_ge(u_made, q.chunk + k + 1)
                f = q.tp + 2 * k
                transposes(f, f % 2, [(u[:, k % 2, t, hl * (P + ROPE):hl * (P + ROPE) + P], hl * T + t * P)
                                      for hl in range(2) for t in range(TT)])
                pe.wait_ge(roped, 1 + k + 1)
                transposes(f + 1, (f + 1) % 2, [(qr[:, t].rearrange("p a b -> p (a b)"), t * P)
                                                for t in range(TT)])

            for k in range(8):
                gm_free(q.chunk + k)
                item(q.item + k, q.item + k, cq_hi, cq_lo, k % 2, 0, width=384, total=LT)
                if k:
                    turn_queries(k - 1)
            turn_queries(7)
            reduce_mod(11)

            s = a["heads"]
            pe.wait_ge(tp_free, s.tp)
            for h in range(MH + 2):
                if h < MH:
                    o = ms_open(head_fill(h, False))
                    rope = slice(ROPE * (h % 2), ROPE * (h % 2) + ROPE)
                    for qs, ks, c0 in ((slice(0, P), slice(0, P), 0), (slice(P, T), slice(0, T), P)):
                        v = o[:, c0:c0 + ks.stop]
                        pe.matmul(v, q_t[:, h, qs], k_t[:, h, ks], start=True, stop=False)
                        ins = pe.matmul(v, qr_t[rope, h // 2, qs], kr_t[rope, ks], start=False, stop=True)
                    ins.then_inc(ms_done, 1)
                if 1 <= h <= MH:
                    pe.wait_ge(p_norm, h)
                    f = s.tp + h - 1
                    transposes(f, f % 2, [(probs[:, (h - 1) % 2, b, :], b * P) for b in range(3)])
                if h >= 2:
                    o = ms_open(head_fill(h - 2, True))
                    pe.wait_ge(tp_free, s.tp + h - 1)
                    pe.matmul(o[:, 0:T], mv_sb[:, 0, h - 2, :], p_t[:, 0:2, :].rearrange("p b q -> p (b q)"),
                              start=True, stop=False)
                    pe.matmul(o[:, P:T], mv_sb[:, 1, h - 2, :], p_t[:, 2, :],
                              start=False, stop=True).then_inc(ms_done, 1)
            pe.wait_ge(ms_free, s.ms + 2 * MH)
            section("mla_out", o_hi, o_lo)
            reduce_mod(12)
            ffn(1, "norm5", (13, None, None), (None, None, None))


_INS = ['x', 'c', 'positions', 'mod_w', 'mod_b', 'norm_mix_g', 'norm_ffn_g', 'gla_w_in', 'gla_w_gate2',
        'gla_b_gate', 'gla_head_g', 'gla_w_o', 'kv_norm_g', 'kv_mod_w', 'kv_mod_b', 'mla_w_dkv',
        'mla_kv_norm_g', 'mla_w_ukv', 'mla_w_dq', 'mla_q_norm_g', 'mla_w_uq', 'mla_w_o', 'ffn_w_up',
        'ffn_conv_w', 'ffn_conv_b', 'ffn_w_down', 'final_norm_g']
_OUTS = [((1, 256, 2048), 'float32')]


def kernel(**inputs):
    import numpy as _np
    import concourse.bacc as _bacc
    from concourse import mybir as _mybir
    from concourse.bass_utils import run_bass_kernel_spmd as _run

    nc = _bacc.Bacc("TRN2", target_bir_lowering=False, num_devices=1)
    arrays, args = {}, []
    for name in _INS:
        a = _np.ascontiguousarray(inputs[name])
        arrays[f"in_{name}_dram"] = a
        args.append(nc.dram_tensor(f"in_{name}_dram", a.shape, _mybir.dt.from_np(a.dtype), kind="ExternalInput").ap())
    for i, (shape, dtype) in enumerate(_OUTS):
        dt = _mybir.dt.from_np(_np.dtype(dtype))
        args.append(nc.dram_tensor(f"out_{i}_dram", shape, dt, kind="ExternalOutput").ap())
    yoco_kernel(nc, *args)
    r = _run(nc, [arrays], core_ids=[0])
    got = tuple(r.results[0][f"out_{i}_dram"] for i in range(len(_OUTS)))
    return got[0]
```
